# Optimizing a Trainium2 kernel written in Bass

```python
import jax, jax.numpy as jnp
from jax import lax
import numpy as np

D_MODEL = 1024
BATCH = 1
SEQ = 512
DEPTH = 1

GLA_HEADS = 4
GLA_DK_HEAD = 64
GLA_DV_HEAD = 128
GLA_DK = GLA_HEADS * GLA_DK_HEAD
GLA_DV = GLA_HEADS * GLA_DV_HEAD
GLA_GATE_RANK = 16
GLA_GATE_TAU = 16.0
GLA_CHUNK = 64
SWA_Q_HEADS = 8
SWA_KV_HEADS = 2
SWA_HEAD_DIM = 64
SWA_WINDOW = 128
SWA_BLOCK = 128
SWA_Q_DIM = SWA_Q_HEADS * SWA_HEAD_DIM
SWA_KV_DIM = SWA_KV_HEADS * SWA_HEAD_DIM
POOL_GROUPS = 4
POOL_GROUP_DIM = 128
POOL_DIM = POOL_GROUPS * POOL_GROUP_DIM
POOL_WINDOWS = (2, 4, 8, 16)
N_BRANCHES = 3
D_FF = 2816
CONV_WIDTH = 3
RMS_EPS = 1e-6

SPLIT_SIZES = (GLA_DK, GLA_DK, GLA_DV, GLA_GATE_RANK, GLA_DV,
               SWA_Q_DIM, SWA_KV_DIM, SWA_KV_DIM,
               POOL_DIM,
               N_BRANCHES * D_MODEL)
N_IN = sum(SPLIT_SIZES)
SPLIT_POINTS = tuple(int(v) for v in np.cumsum(SPLIT_SIZES)[:-1])


def rmsnorm(x, gain):
    xf = x.astype(jnp.float32)
    var = jnp.mean(xf * xf, axis=-1, keepdims=True)
    return (xf * lax.rsqrt(var + RMS_EPS) * gain.astype(jnp.float32)).astype(x.dtype)

def gla_mixer(q, k, v, gate_low, r, w_gate_up, b_gate, norm_gain):
    f32 = jnp.float32
    B, T, _ = q.shape
    nc = T // GLA_CHUNK
    logit = gate_low.astype(f32) @ w_gate_up.astype(f32) + b_gate.astype(f32)
    log_alpha = jax.nn.log_sigmoid(logit) / GLA_GATE_TAU

    def to_chunks(t, d):
        return t.astype(f32).reshape(B, nc, GLA_CHUNK, GLA_HEADS, d).transpose(1, 0, 3, 2, 4)

    qc = to_chunks(q, GLA_DK_HEAD) * (GLA_DK_HEAD ** -0.5)
    kc = to_chunks(k, GLA_DK_HEAD)
    vc = to_chunks(v, GLA_DV_HEAD)
    gc = to_chunks(log_alpha, GLA_DK_HEAD)
    causal = jnp.tril(jnp.ones((GLA_CHUNK, GLA_CHUNK), dtype=bool))

    def step(S, inp):
        qi, ki, vi, gi = inp
        b = jnp.cumsum(gi, axis=2)
        diff = b[:, :, :, None, :] - b[:, :, None, :, :]
        decay = jnp.exp(jnp.where(causal[None, None, :, :, None], diff, -jnp.inf))
        attn = jnp.einsum('bhid,bhjd,bhijd->bhij', qi, ki, decay)
        o = jnp.einsum('bhij,bhjv->bhiv', attn, vi) \
            + jnp.einsum('bhid,bhdv->bhiv', qi * jnp.exp(b), S)
        b_last = b[:, :, -1:, :]
        S_new = jnp.exp(b_last[:, :, 0, :])[..., None] * S \
            + jnp.einsum('bhjd,bhjv->bhdv', ki * jnp.exp(b_last - b), vi)
        return S_new, o

    S0 = jnp.zeros((B, GLA_HEADS, GLA_DK_HEAD, GLA_DV_HEAD), f32)
    _, o = lax.scan(step, S0, (qc, kc, vc, gc))
    o = o.transpose(1, 0, 3, 2, 4).reshape(B, T, GLA_HEADS, GLA_DV_HEAD)
    var = jnp.mean(o * o, axis=-1, keepdims=True)
    o = o * lax.rsqrt(var + RMS_EPS) * norm_gain.astype(f32).reshape(GLA_HEADS, GLA_DV_HEAD)
    o = o.reshape(B, T, GLA_DV) * jax.nn.silu(r.astype(f32))
    return o.astype(q.dtype)

def swa_mixer(q, k, v, sinks):
    f32 = jnp.float32
    B, T, _ = q.shape
    nb = T // SWA_BLOCK
    G = SWA_Q_HEADS // SWA_KV_HEADS
    qb = q.astype(f32).reshape(B, nb, SWA_BLOCK, SWA_KV_HEADS, G, SWA_HEAD_DIM) * (SWA_HEAD_DIM ** -0.5)
    kb = k.astype(f32).reshape(B, nb, SWA_BLOCK, SWA_KV_HEADS, SWA_HEAD_DIM)
    vb = v.astype(f32).reshape(B, nb, SWA_BLOCK, SWA_KV_HEADS, SWA_HEAD_DIM)

    def with_prev(t):
        prev = jnp.concatenate([jnp.zeros_like(t[:, :1]), t[:, :-1]], axis=1)
        return jnp.concatenate([prev, t], axis=2)

    kw, vw = with_prev(kb), with_prev(vb)
    s = jnp.einsum('bnqhgd,bnkhd->bnhgqk', qb, kw)
    blk = jnp.arange(nb)[:, None, None] * SWA_BLOCK
    q_pos = blk + jnp.arange(SWA_BLOCK)[None, :, None]
    k_pos = blk - SWA_BLOCK + jnp.arange(2 * SWA_BLOCK)[None, None, :]
    valid = (k_pos <= q_pos) & (q_pos - k_pos < SWA_WINDOW) & (k_pos >= 0)
    s = jnp.where(valid[None, :, None, None], s, -jnp.inf)
    sink = sinks.astype(f32).reshape(1, 1, SWA_KV_HEADS, G, 1, 1)
    m = jnp.maximum(jnp.max(s, axis=-1, keepdims=True), sink)
    p = jnp.exp(s - m)
    denom = jnp.sum(p, axis=-1, keepdims=True) + jnp.exp(sink - m)
    o = jnp.einsum('bnhgqk,bnkhd->bnqhgd', p / denom, vw)
    return o.reshape(B, T, SWA_Q_DIM).astype(q.dtype)

def pool_mixer(u, w_group, scale):
    f32 = jnp.float32
    B, T, _ = u.shape
    uf = u.astype(f32)
    cs = jnp.cumsum(uf, axis=1)
    pos = jnp.arange(1, T + 1, dtype=f32)
    means = []
    for g, w in enumerate(POOL_WINDOWS):
        cg = cs[..., g * POOL_GROUP_DIM:(g + 1) * POOL_GROUP_DIM]
        shifted = jnp.pad(cg, ((0, 0), (w, 0), (0, 0)))[:, :T]
        cnt = jnp.minimum(pos, float(w))
        means.append((cg - shifted) / cnt[None, :, None])
    pooled = jnp.stack(means, axis=2)
    d = pooled - uf.reshape(B, T, POOL_GROUPS, POOL_GROUP_DIM)
    y = jnp.einsum('btgc,gcd->btgd', d, w_group.astype(f32)).reshape(B, T, POOL_DIM)
    return (y * scale.astype(f32)).astype(u.dtype)

def conv_ffn(h, w_up, conv_w, conv_b, w_down):
    T = h.shape[1]
    up = h @ w_up
    padded = jnp.pad(up, ((0, 0), (CONV_WIDTH - 1, 0), (0, 0)))
    conv = conv_b + conv_w[0] * padded[:, 0:T]
    for i in range(1, CONV_WIDTH):
        conv = conv + conv_w[i] * padded[:, i:i + T]
    gate, val = jnp.split(conv, 2, axis=-1)
    return (jax.nn.gelu(gate, approximate=True) * val) @ w_down

def first_inputs(seed: int = 0) -> dict:
    key = jax.random.key(seed)
    ks = jax.random.split(key, 20)
    L = DEPTH

    def nrm(k, shape, scale):
        return jax.random.normal(k, shape, jnp.float32) * scale

    return {
        "x": nrm(ks[0], (BATCH, SEQ, D_MODEL), 1.0),
        "norm_mix_pre": 1.0 + nrm(ks[1], (L, D_MODEL), 0.05),
        "norm_mix_post": 1.0 + nrm(ks[2], (L, D_MODEL), 0.05),
        "norm_ffn_pre": 1.0 + nrm(ks[3], (L, D_MODEL), 0.05),
        "norm_ffn_post": 1.0 + nrm(ks[4], (L, D_MODEL), 0.05),
        "w_in": nrm(ks[5], (L, D_MODEL, N_IN), D_MODEL ** -0.5),
        "gla_w_gate_up": nrm(ks[6], (L, GLA_GATE_RANK, GLA_DK), GLA_GATE_RANK ** -0.5),
        "gla_b_gate": nrm(ks[7], (L, GLA_DK), 0.1),
        "gla_norm": 1.0 + nrm(ks[8], (L, GLA_DV), 0.05),
        "swa_sinks": nrm(ks[9], (L, SWA_Q_HEADS), 0.5),
        "pool_w": nrm(ks[10], (L, POOL_GROUPS, POOL_GROUP_DIM, POOL_GROUP_DIM), POOL_GROUP_DIM ** -0.5),
        "pool_scale": 1.0 + nrm(ks[11], (L, POOL_DIM), 0.05),
        "w_branch_gla": nrm(ks[12], (L, GLA_DV, D_MODEL), GLA_DV ** -0.5),
        "w_branch_swa": nrm(ks[13], (L, SWA_Q_DIM, D_MODEL), SWA_Q_DIM ** -0.5),
        "w_branch_pool": nrm(ks[14], (L, POOL_DIM, D_MODEL), POOL_DIM ** -0.5),
        "w_out": nrm(ks[15], (L, D_MODEL, D_MODEL), D_MODEL ** -0.5),
        "ffn_w_up": nrm(ks[16], (L, D_MODEL, 2 * D_FF), D_MODEL ** -0.5),
        "ffn_conv_w": nrm(ks[17], (L, CONV_WIDTH, 2 * D_FF), CONV_WIDTH ** -0.5),
        "ffn_conv_b": nrm(ks[18], (L, 2 * D_FF), 0.01),
        "ffn_w_down": nrm(ks[19], (L, D_FF, D_MODEL), D_FF ** -0.5),
    }

def first_block(x, norm_mix_pre, norm_mix_post, norm_ffn_pre, norm_ffn_post, w_in,
              gla_w_gate_up, gla_b_gate, gla_norm, swa_sinks, pool_w, pool_scale,
              w_branch_gla, w_branch_swa, w_branch_pool, w_out,
              ffn_w_up, ffn_conv_w, ffn_conv_b, ffn_w_down):
    B, T, _ = x.shape
    for l in range(DEPTH):
        h = rmsnorm(x, norm_mix_pre[l])
        proj = h @ w_in[l]
        (g_q, g_k, g_v, g_low, g_r, s_q, s_k, s_v, p_u, gates) = jnp.split(proj, SPLIT_POINTS, axis=-1)
        y_a = gla_mixer(g_q, g_k, g_v, g_low, g_r, gla_w_gate_up[l], gla_b_gate[l], gla_norm[l]) @ w_branch_gla[l]
        y_b = swa_mixer(s_q, s_k, s_v, swa_sinks[l]) @ w_branch_swa[l]
        y_c = pool_mixer(p_u, pool_w[l], pool_scale[l]) @ w_branch_pool[l]
        gate = jax.nn.sigmoid(gates.reshape(B, T, N_BRANCHES, D_MODEL))
        merged = gate[:, :, 0] * y_a + gate[:, :, 1] * y_b + gate[:, :, 2] * y_c
        x = x + rmsnorm(merged @ w_out[l], norm_mix_post[l])
        h = rmsnorm(x, norm_ffn_pre[l])
        f = conv_ffn(h, ffn_w_up[l], ffn_conv_w[l], ffn_conv_b[l], ffn_w_down[l])
        x = x + rmsnorm(f, norm_ffn_post[l])
    return x


DEPTH_2 = 2

CHUNK = 64
QBLOCK = 128
N_A = DEPTH_2 // 2
N_B = DEPTH_2 - N_A
FOX_HEADS = 16
FOX_HEAD_DIM = 64
FOX_WIDTH = FOX_HEADS * FOX_HEAD_DIM
MLA_HEADS = 16
MLA_NOPE = 128
MLA_ROPE = 64
MLA_V = 128
KV_LORA = 256
Q_LORA = 768
ROPE_THETA = 10000.0
CONV_W = 3
EPS = 1e-6


def rmsnorm_2(x, g):
    xf = x.astype(jnp.float32)
    y = xf * lax.rsqrt(jnp.mean(xf * xf, axis=-1, keepdims=True) + EPS)
    return (y * g.astype(jnp.float32)).astype(x.dtype)

def rope_tables(seq, dtype):
    pos = jnp.arange(seq, dtype=jnp.float32)
    inv = ROPE_THETA ** (-jnp.arange(0, MLA_ROPE, 2, dtype=jnp.float32) / MLA_ROPE)
    ang = pos[:, None] * inv[None, :]
    return jnp.cos(ang).astype(dtype), jnp.sin(ang).astype(dtype)

def apply_rope(x, cos, sin):
    x1, x2 = jnp.split(x, 2, axis=-1)
    return jnp.concatenate([x1 * cos - x2 * sin, x1 * sin + x2 * cos], axis=-1)

def to_blocks(a):
    b, s = a.shape[:2]
    a = a.reshape((b, s // QBLOCK, QBLOCK) + a.shape[2:])
    return jnp.moveaxis(a, 1, 0)

def from_blocks(a):
    a = jnp.moveaxis(a, 0, 1)
    return a.reshape((a.shape[0], a.shape[1] * a.shape[2]) + a.shape[3:])

def fox_mixer(h, w_in, b_f, w_out):
    b, s_len, _ = h.shape
    proj = h @ w_in
    qkv = proj[..., :3 * FOX_WIDTH].reshape(b, s_len, 3, FOX_HEADS, FOX_HEAD_DIM)
    q, k, v = qkv[:, :, 0], qkv[:, :, 1], qkv[:, :, 2]
    logf = jax.nn.log_sigmoid((proj[..., 3 * FOX_WIDTH:] + b_f).astype(jnp.float32))
    cum = jnp.cumsum(logf, axis=1)
    cum_k = jnp.transpose(cum, (0, 2, 1))
    kpos = jnp.arange(s_len)
    scale = FOX_HEAD_DIM ** -0.5

    def block(args):
        i, qi, ci = args
        sc = jnp.einsum('bqhd,bkhd->bhqk', qi, k, preferred_element_type=jnp.float32) * scale
        sc = sc + (jnp.transpose(ci, (0, 2, 1))[..., :, None] - cum_k[:, :, None, :])
        qpos = i * QBLOCK + jnp.arange(QBLOCK)
        sc = jnp.where(kpos[None, :] <= qpos[:, None], sc, -jnp.inf)
        p = jax.nn.softmax(sc, axis=-1).astype(v.dtype)
        return jnp.einsum('bhqk,bkhd->bqhd', p, v)

    o = lax.map(block, (jnp.arange(s_len // QBLOCK), to_blocks(q), to_blocks(cum)))
    return from_blocks(o).reshape(b, s_len, FOX_WIDTH) @ w_out

def mla_shared_kv(x, kv_in_g, w_dkv, kv_norm_g, w_uk, w_uv, cos, sin):
    b, s_len, _ = x.shape
    ckv = rmsnorm_2(x, kv_in_g) @ w_dkv
    latent = rmsnorm_2(ckv[..., :KV_LORA], kv_norm_g)
    k_rope = apply_rope(ckv[..., KV_LORA:], cos, sin)
    k_nope = (latent @ w_uk).reshape(b, s_len, MLA_HEADS, MLA_NOPE)
    v = (latent @ w_uv).reshape(b, s_len, MLA_HEADS, MLA_V)
    return k_nope, k_rope, v

def mla_mixer(h, w_dq, q_norm_g, w_uq, w_out, k_nope, k_rope, v, cos, sin):
    b, s_len, _ = h.shape
    q = (rmsnorm_2(h @ w_dq, q_norm_g) @ w_uq).reshape(b, s_len, MLA_HEADS, MLA_NOPE + MLA_ROPE)
    q_nope = q[..., :MLA_NOPE]
    q_rope = apply_rope(q[..., MLA_NOPE:], cos[:, None, :], sin[:, None, :])
    kpos = jnp.arange(s_len)
    scale = (MLA_NOPE + MLA_ROPE) ** -0.5

    def block(args):
        i, qn, qr = args
        sc = (jnp.einsum('bqhd,bkhd->bhqk', qn, k_nope, preferred_element_type=jnp.float32)
              + jnp.einsum('bqhr,bkr->bhqk', qr, k_rope, preferred_element_type=jnp.float32)) * scale
        qpos = i * QBLOCK + jnp.arange(QBLOCK)
        visible = kpos[None, :] < (qpos[:, None] // CHUNK + 1) * CHUNK
        sc = jnp.where(visible, sc, -jnp.inf)
        p = jax.nn.softmax(sc, axis=-1).astype(v.dtype)
        return jnp.einsum('bhqk,bkhd->bqhd', p, v)

    o = lax.map(block, (jnp.arange(s_len // QBLOCK), to_blocks(q_nope), to_blocks(q_rope)))
    return from_blocks(o).reshape(b, s_len, MLA_HEADS * MLA_V) @ w_out

def conv_ffn_2(h, w_in, conv_w, conv_b, w_out):
    s_len = h.shape[1]
    u = h @ w_in
    up = jnp.pad(u, ((0, 0), (CONV_W - 1, 0), (0, 0)))
    u = conv_b + sum(up[:, j:j + s_len] * conv_w[j] for j in range(CONV_W))
    gate, val = jnp.split(u, 2, axis=-1)
    return (jax.nn.silu(gate) * val) @ w_out

def second_inputs(seed: int = 0) -> dict:
    key = jax.random.key(seed)
    ks = jax.random.split(key, 24)
    f32 = jnp.float32
    res = (2.0 * DEPTH_2) ** -0.5

    def nrm(k, shape, scale):
        return jax.random.normal(k, shape, f32) * scale

    def gain(k, shape):
        return 1.0 + 0.02 * jax.random.normal(k, shape, f32)

    w_fox_in = jnp.concatenate([
        nrm(ks[2], (N_A, D_MODEL, 3 * FOX_WIDTH), D_MODEL ** -0.5),
        nrm(ks[3], (N_A, D_MODEL, FOX_HEADS), 0.1 * D_MODEL ** -0.5)], axis=-1)
    return {
        'x': jax.random.normal(ks[0], (BATCH, SEQ, D_MODEL), f32),
        'fox_norm': gain(ks[1], (N_A, D_MODEL)),
        'w_fox_in': w_fox_in,
        'b_fox_f': jax.random.uniform(ks[4], (N_A, FOX_HEADS), f32, 1.0, 6.0),
        'w_fox_out': nrm(ks[5], (N_A, FOX_WIDTH, D_MODEL), FOX_WIDTH ** -0.5 * res),
        'kv_in_norm': gain(ks[6], (D_MODEL,)),
        'w_dkv': nrm(ks[7], (D_MODEL, KV_LORA + MLA_ROPE), D_MODEL ** -0.5),
        'kv_norm': gain(ks[8], (KV_LORA,)),
        'w_uk': nrm(ks[9], (KV_LORA, MLA_HEADS * MLA_NOPE), KV_LORA ** -0.5),
        'w_uv': nrm(ks[10], (KV_LORA, MLA_HEADS * MLA_V), KV_LORA ** -0.5),
        'mla_norm': gain(ks[11], (N_B, D_MODEL)),
        'w_dq': nrm(ks[12], (N_B, D_MODEL, Q_LORA), D_MODEL ** -0.5),
        'q_norm': gain(ks[13], (N_B, Q_LORA)),
        'w_uq': nrm(ks[14], (N_B, Q_LORA, MLA_HEADS * (MLA_NOPE + MLA_ROPE)), Q_LORA ** -0.5),
        'w_mla_out': nrm(ks[15], (N_B, MLA_HEADS * MLA_V, D_MODEL), (MLA_HEADS * MLA_V) ** -0.5 * res),
        'ffn_norm': gain(ks[16], (DEPTH_2, D_MODEL)),
        'w_ffn_in': nrm(ks[17], (DEPTH_2, D_MODEL, 2 * D_FF), D_MODEL ** -0.5),
        'ffn_conv_w': nrm(ks[18], (DEPTH_2, CONV_W, 2 * D_FF), CONV_W ** -0.5),
        'ffn_conv_b': nrm(ks[19], (DEPTH_2, 2 * D_FF), 0.01),
        'w_ffn_out': nrm(ks[20], (DEPTH_2, D_FF, D_MODEL), D_FF ** -0.5 * res),
        'final_norm': gain(ks[21], (D_MODEL,)),
    }

def second_block(x, fox_norm, w_fox_in, b_fox_f, w_fox_out, kv_in_norm, w_dkv, kv_norm, w_uk, w_uv,
              mla_norm, w_dq, q_norm, w_uq, w_mla_out, ffn_norm, w_ffn_in, ffn_conv_w, ffn_conv_b,
              w_ffn_out, final_norm):
    cos, sin = rope_tables(x.shape[1], x.dtype)
    k_nope = k_rope = v = None
    for layer in range(DEPTH_2):
        if layer < N_A:
            x = x + fox_mixer(rmsnorm_2(x, fox_norm[layer]), w_fox_in[layer], b_fox_f[layer],
                              w_fox_out[layer])
        else:
            if layer == N_A:
                k_nope, k_rope, v = mla_shared_kv(x, kv_in_norm, w_dkv, kv_norm, w_uk, w_uv, cos, sin)
            j = layer - N_A
            x = x + mla_mixer(rmsnorm_2(x, mla_norm[j]), w_dq[j], q_norm[j], w_uq[j], w_mla_out[j],
                              k_nope, k_rope, v, cos, sin)
        x = x + conv_ffn_2(rmsnorm_2(x, ffn_norm[layer]), w_ffn_in[layer], ffn_conv_w[layer],
                         ffn_conv_b[layer], w_ffn_out[layer])
    return rmsnorm_2(x, final_norm)


def setup_inputs(seed=0):
    out = dict(first_inputs(seed))
    for name, value in second_inputs(seed + 1).items():
        if name != "x":
            out[name + "_2"] = value
    return out


def reference(
    x, norm_mix_pre, norm_mix_post, norm_ffn_pre, norm_ffn_post, w_in, gla_w_gate_up,
    gla_b_gate, gla_norm, swa_sinks, pool_w, pool_scale, w_branch_gla, w_branch_swa,
    w_branch_pool, w_out, ffn_w_up, ffn_conv_w, ffn_conv_b, ffn_w_down, fox_norm_2, w_fox_in_2,
    b_fox_f_2, w_fox_out_2, kv_in_norm_2, w_dkv_2, kv_norm_2, w_uk_2, w_uv_2, mla_norm_2,
    w_dq_2, q_norm_2, w_uq_2, w_mla_out_2, ffn_norm_2, w_ffn_in_2, ffn_conv_w_2, ffn_conv_b_2,
    w_ffn_out_2, final_norm_2,
):
    x = first_block(
        x, norm_mix_pre, norm_mix_post, norm_ffn_pre, norm_ffn_post, w_in, gla_w_gate_up,
        gla_b_gate, gla_norm, swa_sinks, pool_w, pool_scale, w_branch_gla, w_branch_swa,
        w_branch_pool, w_out, ffn_w_up, ffn_conv_w, ffn_conv_b, ffn_w_down,
    )
    return second_block(
        x, fox_norm_2, w_fox_in_2, b_fox_f_2, w_fox_out_2, kv_in_norm_2, w_dkv_2, kv_norm_2,
        w_uk_2, w_uv_2, mla_norm_2, w_dq_2, q_norm_2, w_uq_2, w_mla_out_2, ffn_norm_2,
        w_ffn_in_2, ffn_conv_w_2, ffn_conv_b_2, w_ffn_out_2, final_norm_2,
    )


_drawn_inputs = setup_inputs


def setup_inputs(seed=0):
    import zlib

    import numpy as np

    out = dict(_drawn_inputs(seed))
    spreads = {}
    factors = {'gla_b_gate': 2.723,
     'swa_sinks': 6.131,
     'ffn_conv_b': 6.574,
     'fox_norm_2': 8.0,
     'kv_in_norm_2': 8.0,
     'kv_norm_2': 8.0,
     'mla_norm_2': 8.0,
     'q_norm_2': 8.0,
     'ffn_norm_2': 7.84,
     'ffn_conv_b_2': 8.0,
     'final_norm_2': 2.839}
    for name, (base, spread) in spreads.items():
        noise = np.random.default_rng([zlib.crc32(name.encode()), seed]).standard_normal(out[name].shape)
        drawn = base * np.exp(spread * noise) if base else spread * noise
        out[name] = __import__('jax').numpy.asarray(drawn.astype(out[name].dtype))
    for name, factor in factors.items():
        out[name] = (out[name] * factor).astype(out[name].dtype)
    return out
```

```python
from contextlib import ExitStack

import numpy as np

import concourse.bass as bass
from concourse import mybir

ALU = mybir.AluOpType
ACT = mybir.ActivationFunctionType
AX = mybir.AxisListType
F32 = mybir.dt.float32
F32R = mybir.dt.float32r
BF16 = mybir.dt.bfloat16
U8 = mybir.dt.uint8

P = 128
T = 512
NT = T // P
D = 1024
KD = D // P
FF = 2816
KF = FF // P
HALF = KF // 2
EPS = 1e-6
BLOCKS = 16
SLOT = BLOCKS * P

GLA_H, GLA_DK, GLA_CHUNK = 4, 64, 64
NCHUNK = T // GLA_CHUNK
SWA_H, SWA_G = 8, 4
WINDOWS = (2, 4, 8, 16)
PAD = 16
FOX_H = 16
MLA_H = 16
MLA_SCALE = 192 ** -0.5
LORA_K, QLORA_K = 2, 6
LEVELS = (32, 16, 8, 4, 2, 1)
BRANCH_ORDER = (2, 1, 0)
NEG = -1e30
ROWS = ((1, 384, 128), (2, 0, 256), (1, 0, 384), (0, 0, 512))
BY_BANK = ((3,), (2, 0), (1,))
COLS = ((0, 0, 512), (1, 0, 384), (2, 0, 256), (1, 384, 128))


def stage_table():
    rows = [("mix", 12, 23, 23, 16), ("merge", 24, 48, 48, 12), ("wout", 4, 8, 8, 16),
            ("up0", KF, 2 * KF, 2 * KF, 16), ("down0", 16, 16, 8, HALF),
            ("foxf", 1, 1, 1, 8), ("foxv", 4, 8, 8, 16), ("foxp", 8, 16, 16, 16), ("foxo", 4, 8, 8, 16),
            ("up1", KF, 2 * KF, 2 * KF, 16), ("down1", 16, 16, 8, HALF),
            ("ckv", 2, 4, 4, 16), ("dq", 3, 6, 6, 16), ("mlap", 16, 64, 64, 16), ("mlao", 8, 8, 8, 16),
            ("up2", KF, 2 * KF, 2 * KF, 16), ("down2", 16, 16, 8, HALF)]
    table, totals, chunk, group, drain = {}, {}, 0, 0, 0
    for name, chunks, groups, drains, blocks in rows:
        table[name] = (chunk, group, drain, chunks, blocks * P)
        totals[name] = groups
        chunk, group, drain = chunk + chunks, group + groups, drain + drains
    return table, totals, chunk


STAGES, GROUPS, CHUNKS = stage_table()
ORDER = list(STAGES)

PARAM, _at = {}, 0
for _name, _n in [("mixpre", 8), ("mixpost", 8), ("ffnpre0", 8), ("ffnpost", 8), ("fox", 8), ("ffnpre1", 8),
                  ("kvin", 8), ("mla", 8), ("ffnpre2", 8), ("final", 8), ("kvn", 2), ("qn", 6), ("gla", 4),
                  ("bgate", 2), ("bfox", 1), ("sink", 8), ("pscale", 4),
                  ("conv0", KF * 8), ("conv1", KF * 8), ("conv2", KF * 8)]:
    PARAM[_name] = _at
    _at += _n
NPARAM = _at
CONST, _at = {}, 0
for _name, _n in [("ident", P), ("ones", P), ("rot", P), ("sel", FOX_H), ("eps", 1), ("one", 1), ("inv", 4 * PAD)]:
    CONST[_name] = _at
    _at += _n
NCONST = _at


def on_chip_model(nc, xT, weights, params, consts, masks16, masks8, gate_up, pool_w, rope, resets, outT):
    with ExitStack() as ctx:
        def sem(name):
            return ctx.enter_context(nc.semaphore(name))

        class Region:

            def __init__(self, start):
                self.at = start

            def __call__(self, name, shape, dt=F32):
                size = int(np.prod(shape[1:])) * {BF16: 2, U8: 1}.get(dt, 4)
                at = self.at
                self.at = at + (size + 31) // 32 * 32
                assert self.at <= nc.sbuf_usable_end, (name, self.at)
                return nc.alloc_sbuf_tensor_at(name, shape, dt, offset=at)

        keep = Region((nc.sbuf_base + 31) // 32 * 32)
        X = keep("X", [P, KD, T])
        hh_at = keep.at
        HH = keep("HH", [P, KD, T], F32R)
        HL = keep("HL", [P, KD, T], F32R)
        RAW = keep("RAW", [P, 2, SLOT])
        WHI = keep("WHI", [P, 2, SLOT], F32R)
        WLO = keep("WLO", [P, 2, SLOT], F32R)
        PAR = keep("PAR", [P, NPARAM])
        CON = keep("CON", [P, NCONST])
        M16 = keep("M16", [P, 5 * P], BF16)
        POOLW = keep("POOLW", [P, 4, P])
        RSTD = keep("RSTD", [P, T])
        SUMSQ = keep("SUMSQ", [P, T])
        sq_at = keep.at
        SQ = keep("SQ", [P, 2, T])
        RCOL = keep("RCOL", [P, NT])
        NM = keep("NM", [P, 2, NT])
        SUM = keep("SUM", [P, 2, NT])
        RS = keep("RS", [P, 2, NT])
        arena = keep.at

        mix = Region(arena)
        ft_at = mix.at
        FT = mix("FT", [P, 18, T])
        GV = mix("GV", [P, NT, 512])
        SV = mix("SV", [P, NT, P])
        M8 = mix("M8", [P, 7 * P], U8)
        y_at = mix.at
        YH = mix("YH", [P, 12, T], F32R)
        YL = mix("YL", [P, 12, T], F32R)
        F_LOW, F_K, F_Q, F_SK, F_SQ, F_PU, F_R = 0, 1, 3, 5, 6, 10, 14
        Y_GLA, Y_SWA, Y_POOL = 0, 4, 8
        tmp = Region(y_at)
        RESET = tmp("RESET", [P, 2 * T])
        BC = tmp("BC", [P, 2 * T])
        EX = tmp("EX", [P, 2 * T])
        QT = tmp("QT", [P, 2 * T])
        KT = tmp("KT", [P, 2 * T])
        KDT = tmp("KDT", [P, NT, 2 * P])
        GUP = tmp("GUP", [P, 2 * P])
        EBL = tmp("EBL", [P, 2, NCHUNK])
        M8F = nc.alloc_sbuf_tensor_at("M8F", [P, 7 * P], F32, offset=tmp.at)
        M16F = nc.alloc_sbuf_tensor_at("M16F", [P, 5 * P], F32, offset=tmp.at + 7 * P * 4)
        ATT = tmp("ATT", [P, NT, 4, P])
        SALL = tmp("SALL", [P, 2, NCHUNK, P])
        assert tmp.at <= mix.at
        GZ = nc.alloc_sbuf_tensor_at("GZ", [P, 2 * T], F32, offset=ft_at + F_PU * T * 4)
        GL = nc.alloc_sbuf_tensor_at("GL", [P, 2 * T], F32, offset=ft_at + (F_PU + 2) * T * 4)
        late = Region(ft_at)
        RG = late("RG", [P, T])
        GT = late("GT", [P, T])
        PA = late("PA", [P, PAD + T])
        PB = late("PB", [P, PAD + T])
        DIFF = late("DIFF", [P, T])
        assert late.at <= ft_at + F_SQ * T * 4
        SP = nc.alloc_sbuf_tensor_at("SP", [P, 8, 2 * P], F32, offset=y_at + Y_POOL * T * 4)
        SPT = nc.alloc_sbuf_tensor_at("SPT", [P, 4, T], F32, offset=y_at + (12 + Y_POOL) * T * 4)
        small = Region(mix.at)
        MX = small("MX", [P, 8])
        NMX = small("NMX", [P, 8])
        DS = small("DS", [P, 8])
        ES = small("ES", [P, 8])
        SSUM = small("SSUM", [P, 8])
        DEN = small("DEN", [P, 8])

        mer = Region(ft_at)
        MH = mer("MH", [P, KD, T], F32R)
        ML = mer("ML", [P, KD, T], F32R)
        Z = mer("Z", [P, 2, T])
        G = mer("G", [P, 2, T])
        BR = mer("BR", [P, T])
        ACC = mer("ACC", [P, T])
        assert mer.at <= y_at
        FB = nc.alloc_sbuf_tensor_at("FB", [P, KD, T], F32, offset=hh_at)

        ffn = Region(arena)
        ACTH = ffn("ACTH", [P, KF, T], F32R)
        ACTL = ffn("ACTL", [P, KF, T], F32R)
        U = ffn("U", [P, 2, 2 + T])
        CV = ffn("CV", [P, 2, T])

        fox = Region(arena)
        FV = fox("FV", [P, NT, D])
        QA = fox("QA", [P, 2, 2, T])
        KA = fox("KA", [P, 2, 2, T])
        FP = fox("FP", [P, 2, 5 * 2 * P])
        FPT = fox("FPT", [P, 2, 5 * 2 * P])
        foh_at = fox.at
        FOH = fox("FOH", [P, KD, T], F32R)
        FOL = fox("FOL", [P, KD, T], F32R)
        CUM = fox("CUM", [P, T])
        VST = fox("VST", [P, 2, NT, P])
        FZ = nc.alloc_sbuf_tensor_at("FZ", [P, 2, T], F32, offset=foh_at)
        ONES = nc.alloc_sbuf_tensor_at("ONES", [P, T], F32, offset=foh_at + 2 * T * 4)

        mla = Region(arena)
        CQH = mla("CQH", [P, QLORA_K, T], F32R)
        CQL = mla("CQL", [P, QLORA_K, T], F32R)
        LH = mla("LH", [P, LORA_K, T], F32R)
        LL = mla("LL", [P, LORA_K, T], F32R)
        KR = mla("KR", [P, T])
        CS = mla("CS", [P, 2, T])
        QN = mla("QN", [P, 2, T])
        KN = mla("KN", [P, 2, T])
        MV = mla("MV", [P, 2, NT, P])
        QR = mla("QR", [P, T])
        MP = mla("MP", [P, 5 * 2 * P])
        MPT = mla("MPT", [P, 5 * 2 * P])
        RSTDK = mla("RSTDK", [P, T])
        mol_at = mla.at
        MOL = mla("MOL", [P, MLA_H, T], F32R)
        MOH = nc.alloc_sbuf_tensor_at("MOH", [P, MLA_H, T], F32R, offset=hh_at)
        QRS = nc.alloc_sbuf_tensor_at("QRS", [P, T], F32, offset=sq_at)
        RT = nc.alloc_sbuf_tensor_at("RT", [P, T], F32, offset=sq_at + T * 4)
        CKV = nc.alloc_sbuf_tensor_at("CKV", [P, LORA_K, T], F32, offset=mol_at)
        CQ = nc.alloc_sbuf_tensor_at("CQ", [P, QLORA_K, T], F32, offset=mol_at + LORA_K * T * 4)

        ps = ctx.enter_context(nc.psum_tensor("ps", [P, 8, T], F32))

        par_in, w_in, x_in = sem("par_in"), [sem("w_in0"), sem("w_in1")], sem("x_in")
        w_hi, w_lo = sem("w_hi"), sem("w_lo")
        lin_done, drained = sem("lin_done"), sem("drained")
        h_hi, h_lo, sq_done, sumsq, cleared = sem("h_hi"), sem("h_lo"), sem("sq_done"), sem("sumsq"), sem("cleared")
        stat_done, ln_done, rstd_done, x_done = sem("stat_done"), sem("ln_done"), sem("rstd_done"), sem("x_done")
        col_done, col_read = sem("col_done"), sem("col_read")
        g_l, g_z, g_act, g_dve = sem("g_l"), sem("g_z"), sem("g_act"), sem("g_dve")
        g_ex, g_dec, g_lev, g_s, g_sel = sem("g_ex"), sem("g_dec"), sem("g_lev"), sem("g_s"), sem("g_sel")
        g_kd, g_kt, g_kdt, g_ds, g_st, g_qe = (sem(n) for n in ("g_kd", "g_kt", "g_kdt", "g_ds", "g_st", "g_qe"))
        g_o, g_sq, g_ss, g_ln, g_rg, g_silu, g_hi = (
            sem(n) for n in ("g_o", "g_sq", "g_ss", "g_ln", "g_rg", "g_silu", "g_hi"))
        s_s, s_m, s_e, s_p, s_t, s_turned, s_o, s_hi, s_y, s_dve = (
            sem(n) for n in ("s_s", "s_m", "s_e", "s_p", "s_t", "s_turned", "s_o", "s_hi", "s_y", "s_dve"))
        p_dve, p_d, p_o, p_hi, p_y = (sem(n) for n in ("p_dve", "p_d", "p_o", "p_hi", "p_y"))
        gated, mer_dve, merged = sem("gated"), sem("mer_dve"), sem("merged")
        tap, conv_done, act_done, ffn_dve, acts = (sem(n) for n in ("tap", "conv_done", "act_done", "ffn_dve", "acts"))
        post_dve = sem("post_dve")
        a_s, a_m, a_e, a_p, a_t, a_pt, a_o, a_hi, a_rs = (
            sem(n) for n in ("a_s", "a_m", "a_e", "a_p", "a_t", "a_pt", "a_o", "a_hi", "a_rs"))
        f_act, f_dve, f_qk, f_v, f_y = (sem(n) for n in ("f_act", "f_dve", "f_qk", "f_v", "f_y"))
        m_rot, m_dve, lat_hi, lat_done, m_y, cs_in = (
            sem(n) for n in ("m_rot", "m_dve", "lat_hi", "lat_done", "m_y", "cs_in"))
        waited = sem("waited")
        out_done, out_ready = sem("out_done"), sem("out_ready")

        SQ_AT, HH_AT, STAT_AT = {}, {}, {}
        n_sq = n_hh = 0
        for k, (site, squares, tiles) in enumerate(
                [("mixpre", 8, 8), ("mixpost", 8, 0), ("ffnpre0", 8, 8), ("ffnpost", 8, 0), ("fox", 8, 8),
                 ("ffnpre1", 8, 8), ("kvin", 8, 8), ("kvn", 2, 0), ("mla", 0, 8), ("qn", 6, 0), ("ffnpre2", 8, 8),
                 ("final", 8, 0)]):
            SQ_AT[site], HH_AT[site] = n_sq, n_hh
            n_sq, n_hh = n_sq + squares, n_hh + tiles
        for k, site in enumerate(["mixpre", "mixpost", "ffnpre0", "ffnpost", "fox", "ffnpre1", "kvin", "kvn", "qn",
                                  "ffnpre2", "final"]):
            STAT_AT[site] = k
        SITES = list(STAT_AT)

        def par(name, at=0, n=1):
            return PAR[:, bass.ds(PARAM[name] + at, n)]

        def con(name, n=1, at=0):
            return CON[:, CONST[name] + at:CONST[name] + at + n]

        ident, ones = con("ident", P), con("ones", P)

        def tile(t, j):
            return t[:, bass.ds(j, 1), :].rearrange("p a n -> p (a n)")

        class Steps:

            def __init__(self, eng, s, start=0):
                self.eng, self.s, self.n = eng, s, start

            def __call__(self, ins):
                self.n = self.n + 1
                ins.then_inc(self.s, 1)
                self.eng.wait_ge(self.s, self.n)

        def chunk_loop(eng, stage, body):
            first, _, _, n, _ = STAGES[stage]
            with_loop = n // 2 > 1
            if with_loop:
                with eng.Fori(0, n // 2) as i:
                    for k in range(2):
                        body(i * 2 + (first + k), (first + k) % 2, i + (first + k) // 2)
            start = n // 2 * 2 if with_loop else 0
            for k in range(start, n):
                body(first + k, (first + k) % 2, (first + k) // 2)

        block = ctx.enter_context(nc.Block())

        @block.sync
        def _(sp):
            sp.dma_start(PAR[:, :], params).then_inc(par_in, 16)
            sp.dma_start(CON[:, :], consts).then_inc(par_in, 16)
            sp.dma_start(X[:, :, :], xT).then_inc(x_in, 16)
            sp.dma_start(M16F[:, :], masks16).then_inc(par_in, 16)
            sp.dma_start(M8F[:, :], masks8).then_inc(par_in, 16)
            sp.dma_start(POOLW[:, :, :], pool_w).then_inc(par_in, 16)
            sp.dma_start(GUP[0:16, :], gate_up).then_inc(par_in, 16)
            sp.dma_start(RESET[:, :], resets).then_inc(par_in, 16)
            for stage in ORDER:
                cols = STAGES[stage][4]

                def load(c, slot, visit):
                    sp.wait_ge(w_lo, c + 1)
                    sp.dma_start(RAW[:, slot, 0:cols],
                                 weights[bass.ds(c, 1), :, 0:cols].rearrange("a p n -> (a p) n")
                                 ).then_inc(w_in[slot], 16)

                chunk_loop(sp, stage, load)
                if stage == "ckv":
                    sp.wait_ge(drained, 2 + STAGES["ckv"][2])
                    sp.dma_start(CS[:, :, :], rope).then_inc(cs_in, 16)
            sp.wait_ge(out_ready, KD)
            sp.dma_start(outT, X[:, :, :]).then_inc(out_done, 16)
            sp.wait_ge(out_done, 16)

        @block.gpsimd
        def _(pool):
            pool.sem_inc(w_lo, 2)
            for stage in ORDER:
                cols = STAGES[stage][4]

                def lo(c, slot, visit):
                    pool.wait_ge(w_hi, c + 1)
                    pool.tensor_tensor(WLO[:, slot, 0:cols], RAW[:, slot, 0:cols],
                                       WHI[:, slot, 0:cols].bitcast(F32), ALU.subtract).then_inc(w_lo, 1)

                chunk_loop(pool, stage, lo)

        @block.tensor
        def _(pe):
            def split_mm(out, wh, wl, hh, hl, first, last):
                pe.matmul(out, wh, hh, start=first, stop=False)
                pe.matmul(out, wh, hl, start=False, stop=False)
                return pe.matmul(out, wl, hh, start=False, stop=last)

            def chunk_ready(c):
                pe.wait_ge(w_lo, c + 3)

            def group(slot, col, hi, lo, tiles, drain_value, parity, first=True, last=True):
                if first:
                    pe.wait_ge(drained, drain_value + 1)
                for n, k in enumerate(tiles):
                    w = slice(col + n * P, col + (n + 1) * P)
                    mm = split_mm(ps[:, parity, :], WHI[:, slot, w], WLO[:, slot, w], hi[:, k, :], lo[:, k, :],
                                  first and n == 0, last and n == len(tiles) - 1)
                mm.then_inc(lin_done, 1)

            def group_by_token(slot, col, width, hi, lo, tiles, rows, drain_value, parity):
                pe.wait_ge(drained, drain_value + 1)
                for n, r in enumerate(rows):
                    for m, k in enumerate(tiles):
                        w = slice(col + m * width, col + (m + 1) * width)
                        o, q = ps[:, parity, n * width:(n + 1) * width], slice(r * P, (r + 1) * P)
                        pe.matmul(o, hi[:, k, q], WHI[:, slot, w], start=m == 0, stop=False)
                        pe.matmul(o, lo[:, k, q], WHI[:, slot, w], start=False, stop=False)
                        mm = pe.matmul(o, hi[:, k, q], WLO[:, slot, w], start=False, stop=m == len(tiles) - 1)
                mm.then_inc(lin_done, 1)

            def stats(site, n):
                pe.wait_ge(sumsq, SQ_AT[site] + n + 2)
                pe.matmul(ps[:, 7, :], ones, SUMSQ[:, :], start=True, stop=True).then_inc(stat_done, 1)

            def h_ready(site):
                pe.wait_ge(h_lo, HH_AT[site] + KD)

            def two_groups(stage, hi, lo):
                first, _, drain, n, _ = STAGES[stage]
                with pe.Fori(0, n // 2) as i:
                    for k in range(2):
                        chunk_ready(i * 2 + (first + k))
                        for m in range(2):
                            group((first + k) % 2, m * KD * P, hi, lo, range(KD),
                                  i * 4 + (drain + 2 * k + m), (drain + m) % 2)

            pe.wait_ge(par_in, 7 * 16)
            stats("mixpre", 8)
            h_ready("mixpre")
            c0, _, e0, _, _ = STAGES["mix"]
            span = range(KD)

            def mix_group(c, m):
                if m == 0:
                    chunk_ready(c)
                e = e0 + 2 * c + m - (c > 7)
                group(c % 2, m * KD * P, HH, HL, span, e, e % 2)

            def mix_values(c):
                chunk_ready(c)
                for m in range(2):
                    group_by_token(c % 2, 0, 2 * P, HH, HL, span, (2 * m, 2 * m + 1), e0 + 2 * c + m, m)

            def by_token_scale(site):
                pe.wait_ge(rstd_done, STAT_AT[site] + 1)
                for n in range(NT):
                    mm = pe.matmul(ps[:, 7, n:n + 1], RSTD[0:1, n * P:(n + 1) * P], CON[0:1, CONST["ones"]:CONST["ones"] + 1],
                                   start=True, stop=True)
                mm.then_inc(col_done, 1)

            def gla_scores(level):
                if level:
                    pe.wait_ge(g_lev, level)
                for b in range(4):
                    v, rows = b // 2, slice(b // 2 * 64, b // 2 * 64 + 64)
                    if level:
                        pe.wait_ge(g_sel, 4 * (level - 1) + b + 1)
                    elif b < 2:
                        pe.wait_ge(g_z, 2)
                    for n in range(b % 2 * 2, b % 2 * 2 + 2):
                        for a in range(2):
                            if level:
                                at = slice(a * T + n * P, a * T + (n + 1) * P)
                                k_, q_ = KT[rows, at], QT[rows, at]
                            else:
                                k_, q_ = FT[rows, F_K + a, n * P:(n + 1) * P], FT[rows, F_Q + a, n * P:(n + 1) * P]
                            col = (n % 2 * 2 + a) * P
                            mm = pe.matmul(ps[:, 2 + b, col:col + P], k_, q_, start=True, stop=True)
                    mm.then_inc(g_s, 1)

            def gla_turn_keys():
                pe.wait_ge(g_kd, 1)
                for n in range(NT):
                    pe.wait_ge(g_sel, NT * len(LEVELS) + n + 1)
                for n in range(NT):
                    for a in range(2):
                        mm = pe.transpose(ps[:, 2 + n // 2, n % 2 * 256 + a * P:n % 2 * 256 + (a + 1) * P],
                                          KT[:, a * T + n * P:a * T + (n + 1) * P], ident)
                mm.then_inc(g_kt, 1)

            def gla_states():
                pe.wait_ge(g_kdt, 2)
                for c in range(NCHUNK - 1):
                    rows, n = slice(c % 2 * 64, c % 2 * 64 + 64), c // 2
                    for h in range(GLA_H):
                        mm = pe.matmul(ps[h % 2 * 64:h % 2 * 64 + 64, 2 + 2 * (h // 2) + c % 2, c // 2 * P:(c // 2 + 1) * P],
                                       KDT[rows, n, h * 64:(h + 1) * 64], GV[rows, n, h * P:(h + 1) * P],
                                       start=True, stop=True)
                mm.then_inc(g_ds, 1)

            def gla_outputs():
                pe.wait_ge(g_st, 2 * (NCHUNK - 1))
                pe.wait_ge(g_qe, 1)
                for h in range(GLA_H):
                    rows, a = slice(h % 2 * 64, h % 2 * 64 + 64), h // 2
                    for n in range(NT):
                        pe.matmul(ps[:, 2 + h, n * P:(n + 1) * P], GV[:, n, h * P:(h + 1) * P], ATT[:, h % 2 * 2 + n // 2, n % 2 * 2 + a, :],
                                  start=True, stop=False)
                        for c in (2 * n, 2 * n + 1):
                            if c:
                                mm = pe.matmul(ps[:, 2 + h, c * 64:(c + 1) * 64], SALL[rows, a, c, :],
                                               QT[rows, a * T + c * 64:a * T + (c + 1) * 64],
                                               start=False, stop=c == 2 * n + 1)
                    mm.then_inc(g_o, 1)
                for h in range(GLA_H):
                    pe.wait_ge(g_sq, h + 1)
                    if h:
                        pe.wait_ge(g_ln, h)
                    pe.matmul(ps[:, 6, :], ones, SQ[:, h % 2, :], start=True, stop=True).then_inc(g_ss, 1)

            def swa_block(n):
                pe.wait_ge(s_turned, 4 * n) if n else pe.wait_ge(g_hi, 4 * GLA_H)
                for h in range(SWA_H):
                    for b in range(2):
                        at = (h % 2 * 2 + b) * P
                        pe.matmul(ps[:, 2 + h // 2, at:at + P], M16[:, 0:P],
                                  M16[:, (2 if b else 1 if n else 3) * P:][:, 0:P],
                                  start=h % 2 + b == 0, stop=False, skip_group_check=True)
                for h in range(SWA_H):
                    v, g = h // SWA_G, h % SWA_G
                    rows = slice(v * 64, v * 64 + 64)
                    keys = 2 if n else 1
                    mm = pe.matmul(ps[:, 2 + h // 2, h % 2 * 256 + (2 - keys) * P:h % 2 * 256 + 256],
                                   FT[rows, F_SQ + g, n * P:(n + 1) * P],
                                   FT[rows, F_SK, (n + 1 - keys) * P:(n + 1) * P], start=False, stop=True,
                                   skip_group_check=True)
                mm.then_inc(s_s, 1)
                pe.wait_ge(s_p, n + 1)
                for b in range(0 if n else 1, 2):
                    for v in range(2):
                        for g in range(4):
                            mm = pe.transpose(ps[:, 2 + 2 * b + v, g * P:(g + 1) * P],
                                              SP[:, SWA_G * v + g, b * P:(b + 1) * P], ident)
                mm.then_inc(s_t, 1)
                pe.wait_ge(s_turned, 4 * n + 4)
                pe.wait_ge(s_y, n) if n else pe.wait_ge(g_ln, GLA_H)
                for v in range(2):
                    for b in range(0 if n else 1, 2):
                        mm = pe.matmul(ps[v * 64:v * 64 + 64, 6, :], SV[:, n - 1 + b, v * 64:v * 64 + 64],
                                       SPT[:, 2 * b + v, :], start=b == 0 or n == 0, stop=b == 1)
                mm.then_inc(s_o, 1)

            mix_group(0, 0)
            mix_group(0, 1)
            mix_group(1, 0)
            mix_group(1, 1)
            pe.wait_ge(drained, 2 + 1)
            for a in range(2):
                mm = pe.matmul(ps[:, 2 + a, :], GUP[0:16, a * P:(a + 1) * P], FT[0:16, F_LOW, :], start=True, stop=True)
            mm.then_inc(g_l, 1)
            mix_group(2, 0)
            mix_group(2, 1)
            by_token_scale("mixpre")
            mix_values(3)
            mix_values(4)
            pe.wait_ge(drained, 2 + 10)
            gla_scores(0)
            mix_group(5, 0)
            gla_scores(1)
            mix_group(5, 1)
            gla_scores(2)
            mix_group(6, 0)
            gla_scores(3)
            mix_group(6, 1)
            gla_scores(4)
            chunk_ready(7)
            group_by_token(7 % 2, 0, P, HH, HL, span, range(NT), e0 + 14, (e0 + 14) % 2)
            gla_scores(5)
            mix_group(8, 0)
            gla_scores(6)
            mix_group(8, 1)
            gla_turn_keys()
            mix_group(9, 0)
            gla_states()
            mix_group(9, 1)
            mix_group(10, 0)
            mix_group(10, 1)
            mix_group(11, 0)
            mix_group(11, 1)
            gla_outputs()
            for n in range(NT):
                swa_block(n)
            for g in range(4):
                pe.wait_ge(p_d, g + 1)
                pe.wait_ge(p_y, g) if g else pe.wait_ge(s_y, NT)
                pe.matmul(ps[:, 6, :], POOLW[:, g, :], DIFF[:, :], start=True, stop=True).then_inc(p_o, 1)

            c0, _, e0, _, _ = STAGES["merge"]
            pe.wait_ge(p_y, 4)
            with pe.Fori(0, KD // 2) as i:
                for k in range(6):
                    chunk_ready(i * 6 + (c0 + k))
                    b = BRANCH_ORDER[k % 3]
                    e = i * 12 + (e0 + 2 * k)
                    group((c0 + k) % 2, 0, HH, HL, range(KD), e, (e0 + 2 * k) % 2)
                    group((c0 + k) % 2, KD * P, YH, YL, range(4 * b, 4 * b + 4), e + 1, (e0 + 2 * k + 1) % 2)
            pe.wait_ge(merged, 2 * KD)
            two_groups("wout", MH, ML)
            stats("mixpost", 8)
            stats("ffnpre0", 8)

            def ffn(f):
                h_ready(f"ffnpre{f}")
                two_groups(f"up{f}", HH, HL)
                pe.wait_ge(acts, 1 + KF * (f + 1))
                first, _, drain, n, _ = STAGES[f"down{f}"]
                with pe.Fori(0, n // 4) as i:
                    for k in range(4):
                        chunk_ready(i * 4 + (first + k))
                        half = k % 2
                        group((first + k) % 2, 0, ACTH, ACTL, range(half * HALF, (half + 1) * HALF),
                              i * 2 + (drain + k // 2), (drain + k // 2) % 2, half == 0, half == 1)

            ffn(0)
            stats("ffnpost", 8)
            stats("fox", 8)

            def causal_scores(B, pairs, full):
                for tiles in BY_BANK:
                    for i in tiles:
                        bank, col, length = ROWS[i]
                        own = ps[:, B + bank, col + i * P:col + (i + 1) * P]
                        for m, (q_, k_) in enumerate(pairs):
                            pe.matmul(ps[:, B + bank, col:col + length], q_[:, i * P:(i + 1) * P], k_[:, 0:length],
                                      start=m == 0, stop=False)
                        mm = pe.matmul(own, M16[:, 0:P], M16[:, full * P:(full + 1) * P], start=False, stop=True)
                    mm.then_inc(a_s, 1)

            def turn(n, B, probs):
                pe.wait_ge(a_p, n + 1)
                for bank, tiles in ((0, (0,)), (1, (1, 3)), (2, (2,))):
                    for j in tiles:
                        _, col, _ = COLS[j]
                        for i in range(j, NT):
                            rb, rc, _ = ROWS[i]
                            at = rb * T + rc + j * P
                            mm = pe.transpose(ps[:, B + bank, col + (i - j) * P:col + (i - j + 1) * P],
                                              probs[:, at:at + P], ident)
                    mm.then_inc(a_t, 1)

            def weigh(n, out, turned, values):
                pe.wait_ge(a_pt, n * 3 + 3)
                for j in range(NT):
                    bank, col, length = COLS[j]
                    mm = pe.matmul(out[:, j * P:T], values(j), turned[:, bank * T + col:bank * T + col + length],
                                   start=j == 0, stop=j == NT - 1)
                mm.then_inc(a_o, 1)

            h_ready("fox")
            c, _, e, _, _ = STAGES["foxf"]
            chunk_ready(c)
            group(c % 2, 0, HH, HL, range(KD), e, e % 2)
            by_token_scale("fox")
            first, _, drain, n, _ = STAGES["foxv"]
            with pe.Fori(0, n // 2) as i:
                for k in range(2):
                    chunk_ready(i * 2 + (first + k))
                    for m in range(2):
                        group_by_token((first + k) % 2, 0, 2 * P, HH, HL, range(KD), (2 * m, 2 * m + 1),
                                       i * 4 + (drain + 2 * k + m), (drain + m) % 2)
            first, _, drain, n, _ = STAGES["foxp"]

            def fox_group(p, k, m):
                if m == 0:
                    chunk_ready(p + first)
                group((first + k) % 2, m * KD * P, HH, HL, range(KD), p * 2 + (drain + m), (drain + m) % 2)

            def fox_pair(p, r, project):
                for h in range(2):
                    pe.wait_ge(f_qk, p + 1)
                    pe.wait_ge(f_v, p + 1)
                    if h == 0:
                        pe.wait_ge(f_y, p + 1)
                    causal_scores(2 + 3 * h, [(QA[:, r, h, :], KA[:, r, h, :])], 2)
                if project:
                    fox_group(p + 1, r + 1, 0)
                turn(p * 2, 2, FP[:, 0, :])
                if project:
                    fox_group(p + 1, r + 1, 1)
                turn(p * 2 + 1, 5, FP[:, 1, :])
                for h in range(2):
                    weigh(p * 2 + h, ps[64 * h:64 * h + 64, 2, :], FPT[:, h, :],
                          lambda j: VST[:, r, j, 64 * h:64 * h + 64])

            fox_group(0, 0, 0)
            fox_group(0, 0, 1)
            with pe.Fori(0, FOX_H // 4 - 1) as i:
                fox_pair(i * 2, 0, True)
                fox_pair(i * 2 + 1, 1, True)
            fox_pair(FOX_H // 2 - 2, 0, True)
            fox_pair(FOX_H // 2 - 1, 1, False)
            pe.wait_ge(f_y, 1 + FOX_H // 2)
            two_groups("foxo", FOH, FOL)
            stats("ffnpre1", 8)
            ffn(1)
            stats("kvin", 8)
            h_ready("kvin")
            c, _, e, _, _ = STAGES["ckv"]
            chunk_ready(c)
            group(c % 2, 0, HH, HL, range(KD), e, e % 2)
            group(c % 2, KD * P, HH, HL, range(KD), e + 1, (e + 1) % 2)
            chunk_ready(c + 1)
            group((c + 1) % 2, 0, HH, HL, range(KD), e + 2, e % 2)
            pe.wait_ge(drained, e + 2 + 3)
            pe.matmul(ps[:, (e + 3) % 2, :], con("rot", P), QRS[:, :], start=True, stop=True).then_inc(lin_done, 1)
            stats("kvn", 2)
            pe.wait_ge(rstd_done, STAT_AT["kvn"] + 1)
            for n in range(NT):
                mm = pe.matmul(ps[:, 7, n:n + 1], RSTDK[0:1, n * P:(n + 1) * P],
                               CON[0:1, CONST["ones"]:CONST["ones"] + 1], start=True, stop=True)
            mm.then_inc(col_done, 1)
            h_ready("mla")
            c, _, e, n, _ = STAGES["dq"]
            for k in range(n):
                chunk_ready(c + k)
                for m in range(2):
                    group((c + k) % 2, m * KD * P, HH, HL, range(KD), e + 2 * k + m, (e + m) % 2)
            pe.wait_ge(col_read, 3)
            stats("qn", 6)
            pe.wait_ge(lat_done, LORA_K + QLORA_K)
            first, _, drain, _, _ = STAGES["mlap"]

            def head_group(p, odd, what):
                slot = (first + odd) % 2
                order = ("qn", "kn", "v") if odd else ("qn", "qr", "kn", "rot", "v")
                m = order.index(what) + 5 * odd
                blocks = {"qn": 0, "qr": 6} | ({"kn": 6, "v": 8} if odd else {"kn": 12, "v": 14})
                e = p * 8 + (drain + m)
                bank = (drain + m) % 2
                if what == "qn":
                    chunk_ready(p * 2 + (first + odd))
                if what in ("qn", "qr"):
                    group(slot, blocks[what] * P, CQH, CQL, range(QLORA_K), e, bank)
                elif what == "kn":
                    group(slot, blocks[what] * P, LH, LL, range(LORA_K), e, bank)
                elif what == "v":
                    group_by_token(slot, blocks[what] * P, P, LH, LL, range(LORA_K), range(NT), e, bank)
                else:
                    pe.wait_ge(drained, e + 1)
                    pe.matmul(ps[:, bank, :], con("rot", P), QRS[:, :], start=True, stop=True
                              ).then_inc(lin_done, 1)

            def mla_head(p, odd, project):
                n = p * 2 + odd
                half = slice(64 * odd, 64 * odd + 64)
                pe.wait_ge(drained, p * 8 + (drain + (8 if odd else 5) + 2))
                pe.wait_ge(m_rot, p + 2)
                pe.wait_ge(m_y, n + 1)
                causal_scores(2 + 3 * odd, [(QN[:, odd, :], KN[:, odd, :]), (QR[half, :], KR[half, :])], 4)
                nxt = 1 - odd
                if project:
                    head_group(p + odd, nxt, "qn")
                    head_group(p + odd, nxt, "kn" if nxt else "qr")
                turn(n + FOX_H, 2 + 3 * odd, MP[:, :])
                if project:
                    for what in (("v",) if nxt else ("kn", "rot", "v")):
                        head_group(p + odd, nxt, what)
                weigh(n + FOX_H, ps[:, 2 + 3 * odd, :], MPT[:, :], lambda j: MV[:, odd, j, :])

            for what in ("qn", "qr", "kn", "rot", "v"):
                head_group(0, 0, what)
            with pe.Fori(0, MLA_H // 2 - 1) as p:
                mla_head(p, 0, True)
                mla_head(p, 1, True)
            mla_head(MLA_H // 2 - 1, 0, True)
            mla_head(MLA_H // 2 - 1, 1, False)
            pe.wait_ge(m_y, 2 + MLA_H)
            first, _, drain, n, _ = STAGES["mlao"]
            with pe.Fori(0, n // 2) as i:
                for k in range(2):
                    chunk_ready(i * 2 + (first + k))
                    group((first + k) % 2, 0, MOH, MOL, range(MLA_H), i * 2 + (drain + k), (drain + k) % 2)
            stats("ffnpre2", 8)
            ffn(2)
            stats("final", 8)

        @block.scalar
        def _(act):
            def hi(c, slot, visit, cols, freed=None):
                act.wait_ge(w_in[slot], (visit + 1) * 16)
                if freed is not None:
                    act.wait_ge(lin_done, freed)
                act.activation(WHI[:, slot, 0:cols], RAW[:, slot, 0:cols], ACT.Copy).then_inc(w_hi, 1)

            def apart():
                act.sem_inc(waited, 1)

            def next_of(stage):
                at = ORDER.index(stage) + 1
                return STAGES[ORDER[at]][4] if at < len(ORDER) else None

            def stream(stage, turns, groups, body, last_freed=None):
                first, g0, _, n, cols = STAGES[stage]
                per, total = len(groups), None
                assert turns * per == n

                def one(i, k, width):
                    if width is not None:
                        c = first + k + 1
                        hi(i * per + c, c % 2, i * (per // 2) + c // 2 if per % 2 == 0 else (i * per + c) // 2, width,
                           i * (GROUPS[stage] // turns) + (g0 + groups[k]))
                    body(i, k)

                if turns > 1:
                    with act.Fori(0, turns - 1) as i:
                        for k in range(per):
                            one(i, k, cols)
                for k in range(per):
                    one(turns - 1, k, cols if k < per - 1 else next_of(stage))

            def root(site, n, target):
                at = STAT_AT[site]
                act.wait_ge(stat_done, at + 1)
                act.activation(target[:, :], ps[:, 7, :], ACT.Ln, bias=con("eps"), scale=1.0 / n).then_inc(ln_done, 1)
                act.wait_ge(ln_done, at + 1)
                act.activation(target[:, :], target[:, :], ACT.Exp, scale=-0.5).then_inc(rstd_done, 1)

            def square(j, slot, source, site):
                act.wait_ge(sumsq, j + (SQ_AT[site] + 1))
                apart()
                act.activation(SQ[:, slot, :], source, ACT.Square).then_inc(sq_done, 1)

            def h_tile(j, slot, gain, site, squares=True):
                apart()
                act.activation(tile(HH, j), tile(X, j), ACT.Copy, scale=par(gain, j)).then_inc(h_hi, 1)
                if squares:
                    square(j, slot, tile(X, j), site)

            def each_tile(body, n=KD):
                with act.Fori(0, n // 2) as i:
                    for k in range(2):
                        body(i * 2 + k, k)

            act.wait_ge(par_in, 16 * 7)
            act.wait_ge(x_in, 16)
            for j in range(KD):
                h_tile(j, j % 2, "mixpre", "mixpre")
                if j == 1:
                    hi(0, 0, 0, SLOT)
                    hi(1, 1, 0, SLOT)
            root("mixpre", D, RSTD)

            def cast(c):
                done = 2 * (c - 1) - (c - 2 >= 7)
                hi(c, c % 2, c // 2, SLOT if c < 12 else next_of("mix"), done)

            def gla_level(level):
                act.wait_ge(g_ex, level)
                act.activation(EX[:, :], EX[:, :], ACT.Exp).then_inc(g_dec, 1)

            cast(2)
            act.wait_ge(g_z, 2)
            act.activation(GL[:, :], GZ[:, :], ACT.Abs).then_inc(g_act, 1)
            act.wait_ge(g_act, 1)
            act.activation(GL[:, :], GL[:, :], ACT.Exp, scale=-1.0).then_inc(g_act, 1)
            act.wait_ge(g_act, 2)
            act.activation(GL[:, :], GL[:, :], ACT.Ln, bias=con("one")).then_inc(g_act, 1)
            cast(3)
            cast(4)
            cast(5)
            gla_level(1)
            cast(6)
            gla_level(2)
            gla_level(3)
            cast(7)
            gla_level(4)
            cast(8)
            gla_level(5)
            cast(9)
            gla_level(6)
            act.wait_ge(g_dve, 2)
            act.activation(EBL[:, :, :], BC[:, :].rearrange("p (a c s) -> p a c s", a=2, s=GLA_CHUNK)[:, :, :, GLA_CHUNK - 1],
                           ACT.Exp).then_inc(g_act, 1)
            gla_level(7)
            cast(10)
            act.wait_ge(g_kd, 1)
            act.activation(EX[:, :], BC[:, :], ACT.Exp).then_inc(g_dec, 1)
            cast(11)
            act.wait_ge(drained, 2 + 23)
            act.activation(FT[:, F_R:F_R + 4, :], FT[:, F_R:F_R + 4, :], ACT.Silu).then_inc(g_silu, 1)
            cast(12)
            def head_square(h):
                act.wait_ge(g_o, h + 1)
                if h >= 2:
                    act.wait_ge(g_ss, h - 1)
                act.activation(SQ[:, h % 2, :], ps[:, 2 + h, :], ACT.Square).then_inc(g_sq, 1)

            head_square(0)
            head_square(1)
            for h in range(GLA_H):
                act.wait_ge(g_ss, h + 1)
                if h:
                    act.wait_ge(g_hi, 4 * h)
                act.activation(RG[:, :], ps[:, 6, :], ACT.Ln, bias=con("eps"), scale=1.0 / P).then_inc(g_ln, 1)
                act.wait_ge(g_ln, h + 1)
                act.activation(RG[:, :], RG[:, :], ACT.Exp, scale=-0.5).then_inc(g_rg, 1)
                if h + 2 < GLA_H:
                    head_square(h + 2)

            for n in range(NT):
                act.wait_ge(s_m, 2 * n + 2)
                for h in range(8):
                    act.activation(SP[:, h, :], ps[:, 2 + h // 2, h % 2 * 256:(h % 2 + 1) * 256], ACT.Exp,
                                   bias=NMX[:, h:h + 1], accum_out=SSUM[:, h:h + 1])
                act.activation(ES[:, :], DS[:, :], ACT.Exp).then_inc(s_e, 1)
                act.wait_ge(s_t, n + 1)
                for t in range(0 if n else 2, 4):
                    last = act.activation(SPT[:, t, :], ps[:, 2 + t, :], ACT.Copy)
                    last.then_inc(s_turned, 1 if n else 2)
                act.wait_ge(s_o, n + 1)
                act.activation(YH[:, Y_SWA:Y_SWA + 4, n * P:(n + 1) * P],
                               ps[:, 6, :].rearrange("p (g q) -> p g q", g=4), ACT.Copy).then_inc(s_hi, 1)
            for g in range(4):
                act.wait_ge(p_o, g + 1)
                act.activation(YH[:, Y_POOL + g, :], ps[:, 6, :], ACT.Copy, scale=par("pscale", g)).then_inc(p_hi, 1)

            e0 = STAGES["merge"][2]

            def gate(i, k):
                act.wait_ge(drained, i * 12 + (e0 + 2 * k + 3))
                act.activation(G[:, k % 2, :], Z[:, k % 2, :], ACT.Sigmoid).then_inc(gated, 1)

            stream("merge", KD // 2, (0, 2, 4, 6, 8, 10), gate)
            e0 = STAGES["wout"][2]

            def fb_squares(i, k):
                for m in range(2):
                    j = i * 4 + (2 * k + m)
                    act.wait_ge(drained, i * 4 + (e0 + 2 * k + m + 3))
                    square(j, m, tile(FB, j), "mixpost")

            stream("wout", 2, (0, 2), fb_squares)
            root("mixpost", D, RSTD)
            each_tile(lambda j, k: (act.wait_ge(x_done, j + 1), h_tile(j, k, "ffnpre0", "ffnpre0")))
            root("ffnpre0", D, RSTD)

            def ffn(f, down_body):
                e0 = STAGES[f"up{f}"][2]
                func = ACT.Gelu_apprx_tanh if f == 0 else ACT.Silu

                def taps(i, k):
                    q = i * 2 + k
                    act.wait_ge(acts, q + (KF * f + 1))
                    for m in range(2):
                        at = q * 8 + 4 * m
                        act.wait_ge(drained, q * 2 + (e0 + m + 3))
                        apart()
                        act.activation(CV[:, m, :], U[:, m, 2:2 + T], ACT.Identity, bias=par(f"conv{f}", at + 3),
                                       scale=par(f"conv{f}", at + 2)).then_inc(tap, 1)
                    act.wait_ge(conv_done, q + (KF * f + 1))
                    act.activation(CV[:, 0, :], CV[:, 0, :], func).then_inc(act_done, 1)

                stream(f"up{f}", KF // 2, (0, 2), taps)
                stream(f"down{f}", 4, (0, 1, 2, 3), down_body)

            def x_tiles(stage, gain, site):
                e0 = STAGES[stage][2]

                def body(i, k):
                    if k % 2:
                        j = i * 2 + k // 2
                        act.wait_ge(drained, i * 2 + (e0 + k // 2 + 3))
                        if gain is None:
                            square(j, k // 2, tile(X, j), site)
                        else:
                            h_tile(j, k // 2, gain, site)

                return body

            e0 = STAGES["down0"][2]

            def fb_squares_2(i, k):
                if k % 2:
                    j = i * 2 + k // 2
                    act.wait_ge(drained, i * 2 + (e0 + k // 2 + 3))
                    square(j, k // 2, tile(FB, j), "ffnpost")

            ffn(0, fb_squares_2)
            root("ffnpost", D, RSTD)
            each_tile(lambda j, k: (act.wait_ge(x_done, j + (KD + 1)), h_tile(j, k, "fox", "fox")))
            root("fox", D, RSTD)

            def softmax_exp(n, r, B, probs):
                for b, tiles in enumerate(BY_BANK):
                    act.wait_ge(a_m, n * 3 + (b + 1))
                    for i in tiles:
                        bank, col, length = ROWS[i]
                        last = act.activation(probs[:, bank * T + col:bank * T + col + length],
                                              ps[:, B + bank, col:col + length], ACT.Exp, bias=NM[:, r, i:i + 1],
                                              accum_out=SUM[:, r, i:i + 1])
                    last.then_inc(a_e, 1)

            def copy_turned(n, B, turned):
                for b, length in enumerate((T, T, 2 * P)):
                    act.wait_ge(a_t, n * 3 + (b + 1))
                    act.activation(turned[:, b * T:b * T + length], ps[:, B + b, 0:length], ACT.Copy).then_inc(a_pt, 1)

            c, g0, _, _, _ = STAGES["foxf"]
            hi(c + 1, (c + 1) % 2, (c + 1) // 2, SLOT, g0)
            act.wait_ge(f_dve, 1)
            act.activation(FZ[:, 1, :], FZ[:, 0, :], ACT.Abs).then_inc(f_act, 1)
            act.wait_ge(f_act, 1)
            act.activation(FZ[:, 1, :], FZ[:, 1, :], ACT.Exp, scale=-1.0).then_inc(f_act, 1)
            act.wait_ge(f_act, 2)
            act.activation(FZ[:, 1, :], FZ[:, 1, :], ACT.Ln, bias=con("one")).then_inc(f_act, 1)
            stream("foxv", 2, (0, 2), lambda i, k: None)
            first, g0, _, n, _ = STAGES["foxp"]
            e_v = STAGES["foxv"][2] + 8

            def stage_values(p, r):
                apart()
                act.activation(VST[:, r, :, :], FV[:, :, bass.ds(p * P, P)], ACT.Copy).then_inc(f_v, 1)

            def fox_pair(turn_, r, width, last=False):
                p = turn_ * 2 + r
                if width is not None:
                    c = first + r + 2
                    hi(p + (first + 2), c % 2, turn_ + c // 2, width, p * 2 + (g0 + 2))
                if not last:
                    stage_values(p + 1, 1 - r)
                for h in range(2):
                    softmax_exp(p * 2 + h, h, 2 + 3 * h, FP[:, h, :])
                for h in range(2):
                    copy_turned(p * 2 + h, 2 + 3 * h, FPT[:, h, :])
                act.wait_ge(a_o, p * 2 + 2)
                apart()
                act.activation(tile(FOH, p), ps[:, 2, :], ACT.Copy).then_inc(a_hi, 1)

            c = first + 1
            hi(c, c % 2, c // 2, SLOT, g0)
            act.wait_ge(drained, 2 + e_v)
            stage_values(0, 0)
            with act.Fori(0, FOX_H // 4 - 1) as i:
                fox_pair(i, 0, SLOT)
                fox_pair(i, 1, SLOT)
            fox_pair(FOX_H // 4 - 1, 0, next_of("foxp"))
            fox_pair(FOX_H // 4 - 1, 1, None, True)
            e0 = STAGES["foxo"][2]

            def out_tiles(i, k):
                for m in range(2):
                    j = i * 4 + (2 * k + m)
                    act.wait_ge(drained, i * 4 + (e0 + 2 * k + m + 3))
                    h_tile(j, m, "ffnpre1", "ffnpre1")

            stream("foxo", 2, (0, 2), out_tiles)
            root("ffnpre1", D, RSTD)
            ffn(1, x_tiles("down1", "kvin", "kvin"))
            root("kvin", D, RSTD)

            def latent_tiles(source, target, gain, e, n):
                for j in range(n):
                    act.wait_ge(drained, e + j + 3)
                    act.activation(target[:, j, :], source[:, j, :], ACT.Copy, scale=par(gain, j)).then_inc(lat_hi, 1)
                    square(j, (SQ_AT[gain] + j) % 2, source[:, j, :], gain)

            c, g0, _, _, _ = STAGES["ckv"]
            hi(c + 1, (c + 1) % 2, (c + 1) // 2, SLOT, g0)
            latent_tiles(CKV, LH, "kvn", STAGES["ckv"][2], LORA_K)
            hi(c + 2, (c + 2) % 2, (c + 2) // 2, SLOT, g0 + 2)
            root("kvn", LORA_K * P, RSTDK)
            for j in range(KD):
                if j == 0:
                    act.wait_ge(lin_done, g0 + 3)
                act.activation(HH[:, j, :], X[:, j, :], ACT.Copy, scale=par("mla", j)).then_inc(h_hi, 1)
            c, g0, _, _, _ = STAGES["dq"]
            for k in range(3):
                hi(c + k + 1, (c + k + 1) % 2, (c + k + 1) // 2, SLOT, g0 + 2 * k)
                for m in range(2):
                    j = 2 * k + m
                    act.wait_ge(drained, STAGES["dq"][2] + j + 3)
                    act.activation(CQH[:, j, :], CQ[:, j, :], ACT.Copy, scale=par("qn", j)).then_inc(lat_hi, 1)
                    square(j, (SQ_AT["qn"] + j) % 2, CQ[:, j, :], "qn")
            root("qn", QLORA_K * P, RSTD)
            first, g0, _, _, _ = STAGES["mlap"]

            def mla_head(p, odd, width):
                n = p * 2 + odd
                if width is not None:
                    c = first + 2 + odd
                    hi(n + (first + 2), c % 2, p + c // 2, width, p * 8 + (g0 + (8 if odd else 5)))
                softmax_exp(n + FOX_H, odd, 2 + 3 * odd, MP[:, :])
                copy_turned(n + FOX_H, 2 + 3 * odd, MPT[:, :])
                act.wait_ge(a_o, n + (FOX_H + 1))
                apart()
                act.activation(tile(MOH, n), ps[:, 2 + 3 * odd, :], ACT.Copy).then_inc(a_hi, 1)

            c = first + 1
            hi(c, c % 2, c // 2, SLOT, g0)
            with act.Fori(0, MLA_H // 2 - 1) as p:
                mla_head(p, 0, SLOT)
                mla_head(p, 1, SLOT)
            mla_head(MLA_H // 2 - 1, 0, next_of("mlap"))
            mla_head(MLA_H // 2 - 1, 1, None)
            e0 = STAGES["mlao"][2]

            def out_tiles_2(i, k):
                act.wait_ge(drained, i * 2 + (e0 + k + 3))
                square(i * 2 + k, k, tile(X, i * 2 + k), "ffnpre2")

            stream("mlao", 4, (0, 1), out_tiles_2)
            act.wait_ge(lin_done, STAGES["up2"][1])
            each_tile(lambda j, k: act.activation(tile(HH, j), tile(X, j), ACT.Copy, scale=par("ffnpre2", j)
                                                  ).then_inc(h_hi, 1))
            root("ffnpre2", D, RSTD)
            ffn(2, x_tiles("down2", None, "final"))
            root("final", D, RSTD)

        @block.vector
        def _(dve):
            dve.sem_inc(drained, 2)
            dve.sem_inc(sumsq, 2)
            dve.sem_inc(acts, 1)
            dve.sem_inc(f_y, 1)
            dve.sem_inc(m_y, 2)
            clears = [0]

            def mul(out, a, b):
                return dve.tensor_tensor(out, a, b, ALU.mult)

            def stt(out, a, scalar, b, op0, op1):
                return dve.scalar_tensor_tensor(out, a, scalar, b, op0, op1)

            def clear_sum(site):
                if STAT_AT[site]:
                    dve.wait_ge(stat_done, STAT_AT[site])
                dve.memset(SUMSQ[:, :], 0.0).then_inc(cleared, 1)
                dve.wait_ge(cleared, STAT_AT[site] + 1)

            def add_square(j, slot, site):
                dve.wait_ge(sq_done, j + (SQ_AT[site] + 1))
                dve.wait_ge(sumsq, j + (SQ_AT[site] + 2))
                dve.tensor_tensor(SUMSQ[:, :], SUMSQ[:, :], SQ[:, slot, :], ALU.add).then_inc(sumsq, 1)

            def lo_tile(j, gain, site):
                dve.wait_ge(h_hi, j + (HH_AT[site] + 1))
                stt(tile(HL, j), tile(X, j), par(gain, j), tile(HH, j).bitcast(F32), ALU.mult, ALU.subtract
                    ).then_inc(h_lo, 1)

            def scale_known(site):
                dve.wait_ge(rstd_done, STAT_AT[site] + 1)

            def product(e):
                dve.wait_ge(lin_done, e)

            def each_tile(body, n=KD):
                with dve.Fori(0, n // 2) as i:
                    for k in range(2):
                        body(i * 2 + k, k)

            clear_sum("mixpre")
            dve.wait_ge(par_in, 16 * 7)
            dve.tensor_copy(M8[:, :], M8F[:, :])
            dve.tensor_copy(M16[:, :], M16F[:, :])
            dve.wait_ge(x_in, 16)
            for j in range(KD):
                lo_tile(j, "mixpre", "mixpre")
                add_square(j, j % 2, "mixpre")
            scale_known("mixpre")

            def drain(e, out, factor=None):
                dve.wait_ge(lin_done, e + 1)
                if factor is None:
                    mul(out, ps[:, e % 2, :], RSTD[:, :]).then_inc(drained, 1)
                else:
                    stt(out, ps[:, e % 2, :], factor, RSTD[:, :], ALU.mult, ALU.mult).then_inc(drained, 1)

            def col_scale(count):
                dve.wait_ge(col_done, count)
                dve.tensor_copy(RCOL[:, :], ps[:, 7, 0:NT]).then_inc(col_read, 1)
                dve.wait_ge(col_read, count)

            def drain_by_token(e, bank, out, rows, width, rcol):
                n = rows[1] - rows[0]
                mul(out, ps[:, bank, :].rearrange("p (n w) -> p n w", n=n),
                    rcol[:, rows[0]:rows[1]].unsqueeze(2).broadcast_to([P, n, width])).then_inc(drained, 1)

            def exponents(size):
                b = BC[:, :].rearrange("p (n h s) -> p n h s", h=2, s=size)
                x = EX[:, :].rearrange("p (n h s) -> p n h s", h=2, s=size)
                nb = T // size
                mid = b[:, :, 0, size - 1:size].broadcast_to([P, nb, size])
                dve.tensor_tensor(x[:, :, 1, :], b[:, :, 1, :], mid, ALU.subtract)
                return dve.tensor_tensor(x[:, :, 0, :], mid, b[:, :, 0, :], ALU.subtract)

            def select(level):
                for b in range(4):
                    dve.wait_ge(g_s, 4 * level + b + 1)
                    m = M8[:, level * P:(level + 1) * P].unsqueeze(1).broadcast_to([P, 4, P])
                    dve.copy_predicated(ATT[:, b, :, :], m, ps[:, 2 + b, :].rearrange("p (x i) -> p x i", x=4)
                                        ).then_inc(g_sel, 1)

            def operands(level):
                dve.wait_ge(g_dec, level)
                if level > 1:
                    dve.wait_ge(g_s, NT * level)
                mul(QT[:, :], EX[:, :], FT[:, F_Q:F_Q + 2, :].rearrange("p a t -> p (a t)"))
                mul(KT[:, :], EX[:, :], FT[:, F_K:F_K + 2, :].rearrange("p a t -> p (a t)")).then_inc(g_lev, 1)

            def next_level(level):
                if level > 1:
                    dve.wait_ge(g_lev, level - 1)
                exponents(LEVELS[level - 1]).then_inc(g_ex, 1)
                operands(level)

            drain(0, FT[:, F_LOW, :])
            drain(1, FT[:, F_SK, :])
            drain(2, FT[:, F_K, :])
            drain(3, FT[:, F_K + 1, :])
            dve.wait_ge(g_l, 1)
            for a in range(2):
                dve.tensor_scalar(GZ[:, a * T:(a + 1) * T], ps[:, 2 + a, :], par("bgate", a), None, ALU.add
                                  ).then_inc(g_z, 1)
            drain(4, FT[:, F_Q, :], 0.125)
            drain(5, FT[:, F_Q + 1, :], 0.125)
            dve.wait_ge(g_act, 3)
            stt(GZ[:, :], GZ[:, :], 0.0, GL[:, :], ALU.min, ALU.subtract).then_inc(g_dve, 1)
            dve.memset(ATT[:, :, :, :], 0.0)
            dve.wait_ge(g_dve, 1)
            dve.tensor_scalar(GL[:, :], GZ[:, :], 1.0 / 16, None, ALU.mult).then_inc(g_dve, 1)
            dve.wait_ge(g_dve, 2)
            dve.tensor_tensor_scan(BC[:, :], RESET[:, :], GL[:, :], 0.0, ALU.mult, ALU.add).then_inc(g_dve, 1)
            col_scale(1)
            for e in range(6, 10):
                rows = (0, 2) if e % 2 == 0 else (2, 4)
                dve.wait_ge(lin_done, e + 1)
                drain_by_token(e, e % 2, GV[:, rows[0]:rows[1], (e - 6) // 2 * 256:(e - 6) // 2 * 256 + 256], rows, 256, RCOL)
            dve.wait_ge(g_dve, 3)
            next_level(1)
            select(0)
            drain(10, FT[:, F_SQ, :], 0.125)
            select(1)
            next_level(2)
            drain(11, FT[:, F_SQ + 1, :], 0.125)
            select(2)
            next_level(3)
            drain(12, FT[:, F_SQ + 2, :], 0.125)
            select(3)
            next_level(4)
            drain(13, FT[:, F_SQ + 3, :], 0.125)
            select(4)
            next_level(5)
            dve.wait_ge(lin_done, 15)
            drain_by_token(14, 0, SV[:, :, :], (0, NT), P, RCOL)
            select(5)
            next_level(6)
            drain(15, FT[:, F_PU, :])
            select(6)
            dve.wait_ge(g_lev, 6)
            b = BC[:, :].rearrange("p (c s) -> p c s", s=GLA_CHUNK)
            dve.tensor_tensor(EX[:, :].rearrange("p (c s) -> p c s", s=GLA_CHUNK),
                              b[:, :, GLA_CHUNK - 1:GLA_CHUNK].broadcast_to([P, 2 * NCHUNK, GLA_CHUNK]), b, ALU.subtract
                              ).then_inc(g_ex, 1)
            dve.wait_ge(g_dec, 7)
            dve.wait_ge(g_s, NT * 7)
            mul(KT[:, :], EX[:, :], FT[:, F_K:F_K + 2, :].rearrange("p a t -> p (a t)")).then_inc(g_kd, 1)
            drain(16, FT[:, F_PU + 1, :])
            dve.wait_ge(g_dec, 8)
            mul(QT[:, :], EX[:, :], FT[:, F_Q:F_Q + 2, :].rearrange("p a t -> p (a t)")).then_inc(g_qe, 1)
            dve.wait_ge(g_kt, 1)
            for k in range(2):
                dve.tensor_copy(KDT[:, 2 * k:2 * k + 2, :], ps[:, 2 + k, :].rearrange("p (n f) -> p n f", n=2)
                                ).then_inc(g_kdt, 1)
            drain(17, FT[:, F_PU + 2, :])
            dve.wait_ge(g_ds, 1)
            dve.wait_ge(g_act, 4)
            for c in range(NCHUNK - 1):
                for a in range(2):
                    add = ps[:, 2 + 2 * a + c % 2, c // 2 * P:(c // 2 + 1) * P]
                    if c == 0:
                        ins = dve.tensor_copy(SALL[:, a, 1, :], add)
                    else:
                        dve.wait_ge(g_st, 2 * c - 1 + a)
                        ins = stt(SALL[:, a, c + 1, :], SALL[:, a, c, :], EBL[:, a, c:c + 1], add, ALU.mult, ALU.add)
                    ins.then_inc(g_st, 1)
            for e in range(18, 23):
                drain(e, FT[:, (F_PU + 3 if e == 18 else F_R + e - 19), :])
            dve.wait_ge(g_silu, 1)
            for h in range(GLA_H):
                steps = Steps(dve, g_hi, 4 * h)
                dve.wait_ge(g_rg, h + 1)
                steps(mul(GT[:, :], ps[:, 2 + h, :], RG[:, :]))
                steps(stt(GT[:, :], GT[:, :], par("gla", h), FT[:, F_R + h, :], ALU.mult, ALU.mult))
                steps(dve.tensor_copy(YH[:, Y_GLA + h, :], GT[:, :]))
                steps(dve.tensor_tensor(YL[:, Y_GLA + h, :], GT[:, :], YH[:, Y_GLA + h, :].bitcast(F32), ALU.subtract))

            steps = Steps(dve, s_dve)
            for n in range(NT):
                dve.wait_ge(s_s, n + 1)
                steps(dve.tensor_reduce(MX[:, :], ps[:, 2:6, :].rearrange("p b (v k) -> p (b v) k", v=2), AX.X, ALU.max))
                steps(dve.tensor_tensor(MX[:, :], MX[:, :], par("sink", 0, 8), ALU.max))
                dve.tensor_scalar(NMX[:, :], MX[:, :], -1.0, None, ALU.mult).then_inc(s_m, 1)
                dve.tensor_tensor(DS[:, :], par("sink", 0, 8), MX[:, :], ALU.subtract).then_inc(s_m, 1)
                dve.wait_ge(s_e, n + 1)
                steps(dve.tensor_tensor(DEN[:, :], SSUM[:, :], ES[:, :], ALU.add))
                steps(dve.reciprocal(DEN[:, :], DEN[:, :]))
                mul(SP[:, :, :], SP[:, :, :], DEN[:, :].unsqueeze(2).broadcast_to([P, 8, 2 * P])).then_inc(s_p, 1)
                dve.wait_ge(s_hi, n + 1)
                y = slice(n * P, (n + 1) * P)
                dve.tensor_tensor(YL[:, Y_SWA:Y_SWA + 4, y], ps[:, 6, :].rearrange("p (g q) -> p g q", g=4),
                                  YH[:, Y_SWA:Y_SWA + 4, y].bitcast(F32), ALU.subtract).then_inc(s_y, 1)

            steps = Steps(dve, p_dve)
            dve.memset(PA[:, 0:PAD], 0.0)
            steps(dve.memset(PB[:, 0:PAD], 0.0))
            for g, w in enumerate(WINDOWS):
                u = FT[:, F_PU + g, :]
                a, b, k = PA, PB, 1
                steps(dve.tensor_copy(a[:, PAD:], u))
                while k < w:
                    steps(dve.tensor_tensor(b[:, PAD:], a[:, PAD:], a[:, PAD - k:PAD + T - k], ALU.add))
                    a, b, k = b, a, 2 * k
                if g:
                    dve.wait_ge(p_o, g)
                steps(stt(DIFF[:, :], a[:, PAD:], 1.0 / w, u, ALU.mult, ALU.subtract))
                steps(mul(b[:, PAD:2 * PAD], a[:, PAD:2 * PAD], con("inv", PAD, g * PAD)))
                dve.tensor_tensor(DIFF[:, 0:PAD], b[:, PAD:2 * PAD], u[:, 0:PAD], ALU.subtract).then_inc(p_d, 1)
                dve.wait_ge(p_hi, g + 1)
                stt(YL[:, Y_POOL + g, :], ps[:, 6, :], par("pscale", g), YH[:, Y_POOL + g, :].bitcast(F32),
                    ALU.mult, ALU.subtract).then_inc(p_y, 1)

            _, g0, e0, _, _ = STAGES["merge"]
            with dve.Fori(0, KD // 2) as i:
                steps = Steps(dve, mer_dve, i * 4)
                for k in range(6):
                    dve.wait_ge(lin_done, i * 12 + (g0 + 2 * k + 1))
                    mul(Z[:, k % 2, :], ps[:, (e0 + 2 * k) % 2, :], RSTD[:, :]).then_inc(drained, 1)
                    dve.wait_ge(lin_done, i * 12 + (g0 + 2 * k + 2))
                    dve.wait_ge(gated, i * 6 + (k + 1))
                    target = ACC if k % 3 == 0 else BR
                    mul(target[:, :], ps[:, (e0 + 2 * k + 1) % 2, :], G[:, k % 2, :]).then_inc(drained, 1)
                    dve.wait_ge(drained, i * 12 + (e0 + 2 * k + 4))
                    if k % 3:
                        steps(dve.tensor_tensor(ACC[:, :], ACC[:, :], BR[:, :], ALU.add))
                    if k % 3 == 2:
                        j = i * 2 + k // 3
                        dve.tensor_copy(tile(MH, j), ACC[:, :]).then_inc(merged, 1)
                        dve.wait_ge(merged, j * 2 + 1)
                        dve.tensor_tensor(tile(ML, j), ACC[:, :], tile(MH, j).bitcast(F32), ALU.subtract
                                          ).then_inc(merged, 1)
            def ffn(f):
                g0, e0 = STAGES[f"up{f}"][1:3]
                dve.memset(U[:, :, 0:2], 0.0)
                scale_known(f"ffnpre{f}")
                with dve.Fori(0, KF // 2) as i:
                    steps = Steps(dve, ffn_dve, i * 10 + KF * 5 * f)
                    for k in range(2):
                        q = i * 2 + k
                        for m in range(2):
                            dve.wait_ge(lin_done, q * 2 + (g0 + m + 1))
                            mul(U[:, m, 2:2 + T], ps[:, (e0 + m) % 2, :], RSTD[:, :]).then_inc(drained, 1)
                        for m in range(2):
                            dve.wait_ge(tap, q * 2 + (2 * KF * f + m + 1))
                            at = q * 8 + 4 * m
                            steps(stt(CV[:, m, :], U[:, m, 1:1 + T], par(f"conv{f}", at + 1), CV[:, m, :],
                                      ALU.mult, ALU.add))
                            last = stt(CV[:, m, :], U[:, m, 0:T], par(f"conv{f}", at), CV[:, m, :], ALU.mult, ALU.add)
                            if m == 0:
                                last.then_inc(conv_done, 1)
                            else:
                                steps(last)
                        dve.wait_ge(act_done, q + (KF * f + 1))
                        steps(mul(CV[:, 1, :], CV[:, 0, :], CV[:, 1, :]))
                        steps(dve.tensor_scalar(tile(ACTH, q), CV[:, 1, :], 1.0, None, ALU.mult))
                        dve.tensor_tensor(tile(ACTL, q), CV[:, 1, :], tile(ACTH, q).bitcast(F32), ALU.subtract
                                          ).then_inc(acts, 1)

            def post_norm(site, nxt, done):
                scale_known(site)
                clear_sum(nxt)
                gain = {"mixpost": "mixpost", "ffnpost": "ffnpost"}[site]
                with dve.Fori(0, KD // 2) as i:
                    for k in range(2):
                        j = i * 2 + k
                        stt(tile(FB, j), tile(FB, j), par(gain, j), RSTD[:, :], ALU.mult, ALU.mult).then_inc(post_dve, 1)
                        dve.wait_ge(post_dve, j + (done + 1))
                        dve.tensor_tensor(tile(X, j), tile(X, j), tile(FB, j), ALU.add).then_inc(x_done, 1)
                    for k in range(2):
                        j = i * 2 + k
                        lo_tile(j, nxt, nxt)
                        add_square(j, k, nxt)

            def into_x(stage, site, gain, per):
                g0, e0 = STAGES[stage][1:3]
                clear_sum(site)
                with dve.Fori(0, KD // 2) as i:
                    for k in range(2):
                        j = i * 2 + k
                        dve.wait_ge(lin_done, j * per + (g0 + per))
                        dve.tensor_tensor(tile(X, j), tile(X, j), ps[:, (e0 + k) % 2, :], ALU.add).then_inc(drained, 1)
                        if gain:
                            lo_tile(j, gain, site)
                        add_square(j, k, site)

            g0, e0 = STAGES["wout"][1:3]
            clear_sum("mixpost")
            with dve.Fori(0, KD // 2) as i:
                for k in range(2):
                    j = i * 2 + k
                    dve.wait_ge(lin_done, j + (g0 + 1))
                    dve.tensor_scalar(tile(FB, j), ps[:, (e0 + k) % 2, :], 1.0, None, ALU.mult).then_inc(drained, 1)
                    add_square(j, k, "mixpost")
            post_norm("mixpost", "ffnpre0", 0)

            ffn(0)
            g0, e0 = STAGES["down0"][1:3]
            clear_sum("ffnpost")
            with dve.Fori(0, KD // 2) as i:
                for k in range(2):
                    j = i * 2 + k
                    dve.wait_ge(lin_done, j * 2 + (g0 + 2))
                    dve.tensor_scalar(tile(FB, j), ps[:, (e0 + k) % 2, :], 1.0, None, ALU.mult).then_inc(drained, 1)
                    add_square(j, k, "ffnpost")
            post_norm("ffnpost", "fox", KD)

            def row_maxima(n, r, B):
                for b, tiles in enumerate(BY_BANK):
                    dve.wait_ge(a_s, n * 3 + (b + 1))
                    for i in tiles:
                        bank, col, length = ROWS[i]
                        last = dve.tensor_reduce(NM[:, r, i:i + 1], ps[:, B + bank, col:col + length], AX.X, ALU.max,
                                                 negate=True)
                    last.then_inc(a_m, 1)

            def normalise(n, r, probs):
                dve.wait_ge(a_e, n * 3 + 3)
                dve.reciprocal(RS[:, r, :], SUM[:, r, :]).then_inc(a_rs, 1)
                dve.wait_ge(a_rs, n + 1)
                for i in range(NT):
                    bank, col, length = ROWS[i]
                    at = probs[:, bank * T + col:bank * T + col + length]
                    last = dve.tensor_scalar(at, at, RS[:, r, i:i + 1], None, ALU.mult)
                last.then_inc(a_p, 1)

            scale_known("fox")
            g, e = STAGES["foxf"][1:3]
            dve.wait_ge(lin_done, g + 1)
            mul(FZ[:, 0, :], ps[:, e % 2, :], RSTD[:, :]).then_inc(drained, 1)
            dve.wait_ge(drained, e + 3)
            dve.tensor_scalar(FZ[:, 0, :], FZ[:, 0, :], par("bfox"), None, ALU.add).then_inc(f_dve, 1)
            dve.memset(QA[96:128, :, 0, :], 1.0)
            dve.memset(KA[64:96, :, 0, :], 1.0)
            dve.memset(QA[32:64, :, 1, :], 1.0)
            dve.memset(KA[0:32, :, 1, :], 1.0)
            dve.memset(ONES[:, :], 1.0)
            col_scale(2)
            dve.wait_ge(f_act, 3)
            steps = Steps(dve, f_dve, 1)
            steps(stt(FZ[:, 1, :], FZ[:, 0, :], 0.0, FZ[:, 1, :], ALU.min, ALU.subtract))
            steps(dve.tensor_tensor_scan(CUM[:, :], ONES[:, :], FZ[:, 1, :], 0.0, ALU.mult, ALU.add))
            g0, e0 = STAGES["foxv"][1:3]
            with dve.Fori(0, 2) as i:
                for k in range(2):
                    for m in range(2):
                        dve.wait_ge(lin_done, i * 4 + (g0 + 2 * k + m + 1))
                        drain_by_token(None, (e0 + m) % 2, FV[:, 2 * m:2 * m + 2, bass.ds(i * 512 + k * 256, 256)],
                                       (2 * m, 2 * m + 2), 256, RCOL)
            g0, e0 = STAGES["foxp"][1:3]

            def operand(p, r, m, target, factor, rows):
                dve.wait_ge(lin_done, p * 2 + (g0 + m + 1))
                for h in range(2):
                    half = slice(64 * h, 64 * h + 64)
                    last = stt(target[half, r, h, :], ps[half, (e0 + m) % 2, :], factor, RSTD[half, :],
                               ALU.mult, ALU.mult)
                last.then_inc(drained, 1)
                for h in range(2):
                    s = slice(rows[h], rows[h] + 32)
                    last = dve.tensor_scalar(target[s, r, h, :], CUM[s, :],
                                             CON[s, bass.ds(p * 2 + (CONST["sel"] + h), 1)], None, ALU.mult)
                if m:
                    last.then_inc(f_qk, 1)

            def fox_pair(p, r, project):
                row_maxima(p * 2, 0, 2)
                row_maxima(p * 2 + 1, 1, 5)
                normalise(p * 2, 0, FP[:, 0, :])
                if project:
                    operand(p + 1, 1 - r, 0, QA, 0.125, (64, 0))
                normalise(p * 2 + 1, 1, FP[:, 1, :])
                if project:
                    operand(p + 1, 1 - r, 1, KA, 1.0, (96, 32))
                dve.wait_ge(a_hi, p + 1)
                dve.tensor_tensor(tile(FOL, p), ps[:, 2, :], tile(FOH, p).bitcast(F32), ALU.subtract
                                  ).then_inc(f_y, 1)

            operand(0, 0, 0, QA, 0.125, (64, 0))
            operand(0, 0, 1, KA, 1.0, (96, 32))
            with dve.Fori(0, FOX_H // 4 - 1) as i:
                fox_pair(i * 2, 0, True)
                fox_pair(i * 2 + 1, 1, True)
            fox_pair(FOX_H // 2 - 2, 0, True)
            fox_pair(FOX_H // 2 - 1, 1, False)
            into_x("foxo", "ffnpre1", "ffnpre1", 1)
            ffn(1)
            into_x("down1", "kvin", "kvin", 2)
            g0, e0 = STAGES["ckv"][1:3]
            scale_known("kvin")
            clear_sum("kvn")
            for j in range(LORA_K):
                dve.wait_ge(lin_done, g0 + j + 1)
                mul(CKV[:, j, :], ps[:, (e0 + j) % 2, :], RSTD[:, :]).then_inc(drained, 1)
            for j in range(LORA_K):
                dve.wait_ge(lat_hi, j + 1)
                stt(LL[:, j, :], CKV[:, j, :], par("kvn", j), LH[:, j, :].bitcast(F32), ALU.mult, ALU.subtract
                    ).then_inc(lat_done, 1)
                add_square(j, j % 2, "kvn")
            dve.wait_ge(lin_done, g0 + 3)
            mul(QRS[:, :], ps[:, e0 % 2, :], RSTD[:, :]).then_inc(drained, 1)
            dve.wait_ge(cs_in, 16)
            dve.wait_ge(drained, e0 + 5)
            steps = Steps(dve, m_dve)
            mul(RT[:, :], QRS[:, :], CS[:, 0, :])
            dve.wait_ge(lin_done, g0 + 4)
            mul(KR[:, :], ps[:, (e0 + 3) % 2, :], CS[:, 1, :]).then_inc(drained, 1)
            dve.wait_ge(drained, e0 + 6)
            dve.tensor_tensor(KR[:, :], KR[:, :], RT[:, :], ALU.add).then_inc(m_rot, 1)
            col_scale(3)
            for j in range(KD):
                lo_tile(j, "mla", "mla")
            g0, e0 = STAGES["dq"][1:3]
            clear_sum("qn")
            for j in range(QLORA_K):
                dve.wait_ge(lin_done, g0 + j + 1)
                mul(CQ[:, j, :], ps[:, (e0 + j) % 2, :], RSTD[:, :]).then_inc(drained, 1)
                dve.wait_ge(lat_hi, LORA_K + j + 1)
                stt(CQL[:, j, :], CQ[:, j, :], par("qn", j), CQH[:, j, :].bitcast(F32), ALU.mult, ALU.subtract
                    ).then_inc(lat_done, 1)
                add_square(j, j % 2, "qn")
            scale_known("qn")
            g0, e0 = STAGES["mlap"][1:3]

            def head_drain(p, odd, what):
                order = ("qn", "kn", "v") if odd else ("qn", "qr", "kn", "rot", "v")
                m = order.index(what) + 5 * odd
                src = ps[:, (e0 + m) % 2, :]
                if what == "rot":
                    dve.wait_ge(drained, p * 8 + (e0 + m + 1))
                    mul(RT[:, :], QRS[:, :], CS[:, 0, :])
                dve.wait_ge(lin_done, p * 8 + (g0 + m + 1))
                if what == "qn":
                    stt(QN[:, odd, :], src, MLA_SCALE, RSTD[:, :], ALU.mult, ALU.mult).then_inc(drained, 1)
                elif what == "qr":
                    stt(QRS[:, :], src, MLA_SCALE, RSTD[:, :], ALU.mult, ALU.mult).then_inc(drained, 1)
                elif what == "kn":
                    mul(KN[:, odd, :], src, RSTDK[:, :]).then_inc(drained, 1)
                elif what == "v":
                    drain_by_token(None, (e0 + m) % 2, MV[:, odd, :, :], (0, NT), P, RCOL)
                else:
                    mul(QR[:, :], src, CS[:, 1, :]).then_inc(drained, 1)
                    dve.wait_ge(drained, p * 8 + (e0 + m + 3))
                    dve.tensor_tensor(QR[:, :], QR[:, :], RT[:, :], ALU.add).then_inc(m_rot, 1)

            def mla_head(p, odd, project):
                n, nxt = p * 2 + odd, 1 - odd
                row_maxima(n + FOX_H, odd, 2 + 3 * odd)
                normalise(n + FOX_H, odd, MP[:, :])
                if project:
                    for what in (("qn", "kn", "v") if nxt else ("qn", "qr", "kn", "rot", "v")):
                        head_drain(p + odd, nxt, what)
                dve.wait_ge(a_hi, n + (FOX_H // 2 + 1))
                dve.tensor_tensor(tile(MOL, n), ps[:, 2 + 3 * odd, :], tile(MOH, n).bitcast(F32), ALU.subtract
                                  ).then_inc(m_y, 1)

            for what in ("qn", "qr", "kn", "rot", "v"):
                head_drain(0, 0, what)
            with dve.Fori(0, MLA_H // 2 - 1) as p:
                mla_head(p, 0, True)
                mla_head(p, 1, True)
            mla_head(MLA_H // 2 - 1, 0, True)
            mla_head(MLA_H // 2 - 1, 1, False)
            into_x("mlao", "ffnpre2", None, 1)
            each_tile(lambda j, k: lo_tile(j, "ffnpre2", "ffnpre2"))
            ffn(2)
            into_x("down2", "final", None, 2)
            scale_known("final")
            each_tile(lambda j, k: stt(tile(X, j), tile(X, j), par("final", j), RSTD[:, :], ALU.mult, ALU.mult
                                       ).then_inc(out_ready, 1))


def groups_of(w, cols):
    w = w[:, cols]
    return w.reshape(w.shape[0] // P, P, w.shape[1]).transpose(1, 0, 2).reshape(P, -1)


def weight_chunks(i):
    w_in = i["w_in"][0]
    r = np.arange
    at = np.cumsum([0, 256, 256, 512, 16, 512, 512, 128, 128, 512, 3072])
    q, k, v, low, gate_r, sq, sk, sv, pu, gates = at[:10]
    low_w = np.zeros((D, P), np.float32)
    low_w[:, 0:16] = w_in[:, low:low + 16]
    chunks = [[groups_of(low_w, r(P)), groups_of(w_in, sk + r(P))]]
    chunks += [[groups_of(w_in, c + r(P)), groups_of(w_in, c + P + r(P))] for c in (k, q)]
    chunks += [[groups_of(w_in, c + r(256))] for c in (v, v + 256)]
    head = [np.concatenate([sq + g * 64 + r(64), sq + (SWA_G + g) * 64 + r(64)]) for g in range(4)]
    chunks += [[groups_of(w_in, head[g]), groups_of(w_in, head[g + 1])] for g in (0, 2)]
    chunks += [[groups_of(w_in, sv + r(P))]]
    chunks += [[groups_of(w_in, c + r(P)), groups_of(w_in, c + P + r(P))]
               for c in (pu, pu + 256, gate_r, gate_r + 256)]
    swa_rows = np.concatenate([h - sq for h in head])
    branches = [i["w_branch_gla"][0], i["w_branch_swa"][0][swa_rows], i["w_branch_pool"][0]]
    for j in range(KD):
        for b in BRANCH_ORDER:
            chunks.append([groups_of(w_in, gates + b * D + j * P + r(P)), groups_of(branches[b], j * P + r(P))])

    def square(w):
        return [[groups_of(w, c * 256 + r(P)), groups_of(w, c * 256 + P + r(P))] for c in range(w.shape[1] // 256)]

    def ffn(up, down):
        out = [[groups_of(up, f * P + r(P)), groups_of(up, FF + f * P + r(P))] for f in range(KF)]
        for j in range(KD):
            whole = groups_of(down, j * P + r(P))
            out += [[whole[:, :HALF * P]], [whole[:, HALF * P:]]]
        return out

    chunks += square(i["w_out"][0])
    chunks += ffn(i["ffn_w_up"][0], i["ffn_w_down"][0])
    fox = i["w_fox_in_2"][0]
    gate = np.zeros((D, P), np.float32)
    for quadrant in range(4):
        gate[:, quadrant * 32:quadrant * 32 + FOX_H] = fox[:, 3 * D:3 * D + FOX_H]
    chunks += [[groups_of(gate, r(P))]]
    chunks += [[groups_of(fox, 2 * D + c * 256 + r(256))] for c in range(4)]
    chunks += [[groups_of(fox, c * P + r(P)), groups_of(fox, D + c * P + r(P))] for c in range(8)]
    chunks += square(i["w_fox_out_2"][0])
    chunks += ffn(i["w_ffn_in_2"][0], i["w_ffn_out_2"][0])
    dkv = i["w_dkv_2"]
    chunks += [[groups_of(dkv, r(P)), groups_of(dkv, P + r(P))],
               [groups_of(dkv, np.concatenate([256 + r(64), 256 + r(64)]))]]
    chunks += square(i["w_dq_2"][0])
    uq, uk, uv = i["w_uq_2"][0], i["w_uk_2"], i["w_uv_2"]
    for p in range(MLA_H // 2):
        a, b = 2 * p, 2 * p + 1
        rot = np.concatenate([a * 192 + P + r(64), b * 192 + P + r(64)])
        chunks += [[groups_of(uq, a * 192 + r(P)), groups_of(uq, rot), groups_of(uk, a * P + r(P)),
                    groups_of(uv, a * P + r(P))],
                   [groups_of(uq, b * 192 + r(P)), groups_of(uk, b * P + r(P)), groups_of(uv, b * P + r(P))]]
    chunks += [[groups_of(i["w_mla_out_2"][0], j * P + r(P))] for j in range(KD)]
    chunks += ffn(i["w_ffn_in_2"][1], i["w_ffn_out_2"][1])
    assert len(chunks) == CHUNKS
    out = np.zeros((CHUNKS, P, SLOT), np.float32)
    for c, parts in enumerate(chunks):
        whole = np.concatenate(parts, axis=1)
        out[c, :, :whole.shape[1]] = whole
    return out


def small_parameters(i):
    out = np.zeros((P, NPARAM), np.float32)

    def put(name, vector):
        v = vector.reshape(-1, P).T
        out[:, PARAM[name]:PARAM[name] + v.shape[1]] = v

    for name, source in [("mixpre", i["norm_mix_pre"]), ("mixpost", i["norm_mix_post"]),
                         ("ffnpre0", i["norm_ffn_pre"]), ("ffnpost", i["norm_ffn_post"]), ("fox", i["fox_norm_2"]),
                         ("ffnpre1", i["ffn_norm_2"][0]), ("kvin", i["kv_in_norm_2"]), ("mla", i["mla_norm_2"]),
                         ("ffnpre2", i["ffn_norm_2"][1]), ("final", i["final_norm_2"]), ("kvn", i["kv_norm_2"]),
                         ("qn", i["q_norm_2"]), ("gla", i["gla_norm"]), ("bgate", i["gla_b_gate"]),
                         ("pscale", i["pool_scale"])]:
        put(name, source)
    for quadrant in range(4):
        out[quadrant * 32:quadrant * 32 + FOX_H, PARAM["bfox"]] = i["b_fox_f_2"][0]
    out[:, PARAM["sink"]:PARAM["sink"] + SWA_H] = i["swa_sinks"][0]
    for f, (w, b) in enumerate([(i["ffn_conv_w"][0], i["ffn_conv_b"][0]), (i["ffn_conv_w_2"][0], i["ffn_conv_b_2"][0]),
                                (i["ffn_conv_w_2"][1], i["ffn_conv_b_2"][1])]):
        taps = np.concatenate([w, b[None]]).reshape(4, 2, KF, P)
        out[:, PARAM[f"conv{f}"]:PARAM[f"conv{f}"] + KF * 8] = taps.transpose(3, 2, 1, 0).reshape(P, KF * 8)
    return out


def constants():
    con = np.zeros((P, NCONST), np.float32)
    con[:, CONST["ident"]:CONST["ident"] + P] = np.eye(P)
    con[:, CONST["ones"]:CONST["ones"] + P] = 1
    con[:, CONST["eps"]] = EPS
    con[:, CONST["one"]] = 1
    row = np.arange(P)
    rot = np.zeros((P, P), np.float32)
    for r in range(P):
        rot[r + 32 if r % 64 < 32 else r - 32, r] = -1 if r % 64 < 32 else 1
    con[:, CONST["rot"]:CONST["rot"] + P] = rot
    for h in range(FOX_H):
        even = h % 2 == 0
        con[(64 if even else 0) + h, CONST["sel"] + h] = 1
        con[(96 if even else 32) + h, CONST["sel"] + h] = -1
    for g, w in enumerate(WINDOWS):
        con[:, CONST["inv"] + g * PAD:CONST["inv"] + (g + 1) * PAD] = np.float32(1) / np.minimum(
            np.arange(1, PAD + 1), w).astype(np.float32)
    q, k = row[:, None], row[None, :]
    masks16 = np.concatenate([np.eye(P), np.where(k > q, 0, NEG), np.where(k <= q, 0, NEG), np.full((P, P), NEG),
                              np.where(k < (q // 64 + 1) * 64, 0, NEG)], axis=1).astype(np.float32)
    key, query = row[:, None], row[None, :]
    levels = [key == query]
    for s in LEVELS:
        levels.append((key // (2 * s) == query // (2 * s)) & (key % (2 * s) < s) & (query % (2 * s) >= s))
    masks8 = np.concatenate(levels, axis=1).astype(np.float32)
    inv = np.float32(10000.0) ** (-np.arange(0, 64, 2, dtype=np.float32) / np.float32(64))
    angle = (np.arange(T, dtype=np.float32)[:, None] * inv[None, :]).astype(np.float32)
    rope = np.stack([np.cos(angle).T[row % 32], np.sin(angle).T[row % 32]], axis=1).astype(np.float32)
    resets = np.tile((np.arange(2 * T) % GLA_CHUNK != 0).astype(np.float32), (P, 1))
    return con, masks16, masks8, rope, resets


def kernel(**inputs):
    import concourse.bacc as bacc
    from concourse.bass_utils import run_bass_kernel_spmd as run

    i = {name: np.asarray(a) for name, a in inputs.items()}
    con, masks16, masks8, rope, resets = constants()
    arrays = {
        "xT": i["x"][0].T.reshape(KD, P, T).transpose(1, 0, 2),
        "weights": weight_chunks(i),
        "params": small_parameters(i),
        "consts": con, "masks16": masks16, "masks8": masks8,
        "gate_up": i["gla_w_gate_up"][0],
        "pool_w": i["pool_w"][0].transpose(1, 0, 2),
        "rope": rope, "resets": resets,
    }
    arrays = {name: np.ascontiguousarray(a) for name, a in arrays.items()}
    nc = bacc.Bacc("TRN2", target_bir_lowering=False, num_devices=1)
    aps = [nc.dram_tensor(name, a.shape, mybir.dt.from_np(a.dtype), kind="ExternalInput").ap()
           for name, a in arrays.items()]
    out = nc.dram_tensor("outT", (P, KD, T), F32, kind="ExternalOutput").ap()
    on_chip_model(nc, *aps, out)
    r = run(nc, [arrays], core_ids=[0])
    y = np.asarray(r.results[0]["outT"])
    return np.ascontiguousarray(y.transpose(2, 1, 0).reshape(1, T, D))
```
